# Optimizing a Trainium2 kernel written in Bass

```python
import math
import jax
import jax.numpy as jnp
from jax import lax
import numpy as np

D_MODEL = 1024
BATCH = 1
SEQ = 512
DEPTH = 1

RMS_EPS = 1e-5
HG_EXPAND = 128
HG_HEADS = D_MODEL // HG_EXPAND
HG_DK = HG_EXPAND
HG_DV = D_MODEL // HG_HEADS
HG_FDIM = HG_HEADS * HG_DK
HG_VW = HG_HEADS * HG_DV
HG_CHUNK = 64
SWA_HEADS = 16
SWA_KV_HEADS = 4
SWA_GROUP = SWA_HEADS // SWA_KV_HEADS
SWA_HEAD_DIM = 64
SWA_QW = SWA_HEADS * SWA_HEAD_DIM
SWA_KW = SWA_KV_HEADS * SWA_HEAD_DIM
SWA_WINDOW = 128
SWA_BLOCK = 128
T5_BUCKETS = 32
T5_MAX_EXACT = 16
T5_MAX_DIST = 128
MEM_LEN = 256
XA_HEADS = 4
XA_HEAD_DIM = D_MODEL // XA_HEADS
N_EXPERTS = 32
TOP_K = 4
D_FF = D_MODEL
SWIGLU_ALPHA = 1.702
SWIGLU_LIMIT = 7.0
MOE_BLOCK = 128
IN_WIDTHS = (HG_FDIM, HG_FDIM, HG_VW, HG_VW, SWA_QW, SWA_KW, SWA_KW, D_MODEL, D_MODEL)
IN_COLS = sum(IN_WIDTHS)

kernel_name = 'hybrid_hgrn2_swa_sink_moe_block'

def rms_norm(x, gain):
    xf = x.astype(jnp.float32)
    y = xf * lax.rsqrt(jnp.mean(xf * xf, axis=-1, keepdims=True) + RMS_EPS)
    return (y * gain.astype(jnp.float32)).astype(x.dtype)

def split_points():
    pts, acc = [], 0
    for w in IN_WIDTHS[:-1]:
        acc += w
        pts.append(acc)
    return pts

def hgrn2_mixer(q, f_logit, i, g, lb, norm_gain):
    B, S, _ = q.shape
    nc = S // HG_CHUNK
    f32 = jnp.float32
    ff = f_logit.astype(f32)
    lbf = lb.astype(f32)
    log_f = jnp.logaddexp(jnp.log(lbf), jnp.log1p(-lbf) + jax.nn.log_sigmoid(ff))
    k = (1.0 - lbf) * jax.nn.sigmoid(-ff)
    qf = jax.nn.silu(q.astype(f32))

    def to_chunks(t, d):
        return t.reshape(B, nc, HG_CHUNK, HG_HEADS, d).transpose(1, 0, 3, 2, 4)

    xs = (to_chunks(qf, HG_DK), to_chunks(k, HG_DK), to_chunks(i.astype(f32), HG_DV), to_chunks(log_f, HG_DK))
    causal = jnp.tril(jnp.ones((HG_CHUNK, HG_CHUNK), dtype=bool))

    def step(state, inp):
        qb, kb, vb, gb = inp
        G = jnp.cumsum(gb, axis=2)
        o_inter = jnp.einsum('bhtk,bhkv->bhtv', qb * jnp.exp(G), state)
        diff = G[:, :, :, None, :] - G[:, :, None, :, :]
        decay = jnp.exp(jnp.where(causal[:, :, None], diff, -jnp.inf))
        attn = jnp.einsum('bhtk,bhsk,bhtsk->bhts', qb, kb, decay)
        o_intra = jnp.einsum('bhts,bhsv->bhtv', attn, vb)
        G_last = G[:, :, -1:, :]
        k_dec = kb * jnp.exp(G_last - G)
        new_state = jnp.exp(G_last[:, :, 0, :])[..., None] * state + jnp.einsum('bhsk,bhsv->bhkv', k_dec, vb)
        return new_state, o_inter + o_intra

    state0 = jnp.zeros((B, HG_HEADS, HG_DK, HG_DV), f32)
    _, o = lax.scan(step, state0, xs)
    o = o.transpose(1, 0, 3, 2, 4).reshape(B, S, HG_HEADS, HG_DV)
    o = rms_norm(o, norm_gain) * jax.nn.silu(g.astype(f32).reshape(B, S, HG_HEADS, HG_DV))
    return o.reshape(B, S, HG_VW).astype(i.dtype)

def t5_bucket(dist):
    n = jnp.maximum(dist, 0)
    nf = jnp.maximum(n, 1).astype(jnp.float32)
    large = T5_MAX_EXACT + (jnp.log(nf / T5_MAX_EXACT) / math.log(T5_MAX_DIST / T5_MAX_EXACT)
                            * (T5_BUCKETS - T5_MAX_EXACT)).astype(jnp.int32)
    large = jnp.minimum(large, T5_BUCKETS - 1)
    return jnp.where(n < T5_MAX_EXACT, n, large)

def swa_mixer(q, k, v, sinks, t5_table):
    B, S, _ = q.shape
    nb = S // SWA_BLOCK
    qb = q.reshape(B, nb, SWA_BLOCK, SWA_KV_HEADS, SWA_GROUP, SWA_HEAD_DIM)
    kr = k.reshape(B, nb, SWA_BLOCK, SWA_KV_HEADS, SWA_HEAD_DIM)
    vr = v.reshape(B, nb, SWA_BLOCK, SWA_KV_HEADS, SWA_HEAD_DIM)

    def with_prev(t):
        prev = jnp.pad(t[:, :-1], ((0, 0), (1, 0), (0, 0), (0, 0), (0, 0)))
        return jnp.concatenate([prev, t], axis=2)

    kb, vb = with_prev(kr), with_prev(vr)
    t_loc = jnp.arange(SWA_BLOCK, dtype=jnp.int32)[:, None]
    s_loc = jnp.arange(2 * SWA_BLOCK, dtype=jnp.int32)[None, :]
    dist = t_loc + SWA_BLOCK - s_loc
    in_band = (dist >= 0) & (dist < SWA_WINDOW)
    key_exists = (jnp.arange(nb)[:, None] > 0) | (s_loc >= SWA_BLOCK)
    mask = in_band[None] & key_exists[:, None, :]
    bias = t5_table.astype(jnp.float32)[t5_bucket(dist)]
    bias = bias.transpose(2, 0, 1).reshape(SWA_KV_HEADS, SWA_GROUP, 1, SWA_BLOCK, 2 * SWA_BLOCK)
    scores = jnp.einsum('bnqhgd,bnkhd->bhgnqk', qb, kb).astype(jnp.float32) * (SWA_HEAD_DIM ** -0.5) + bias
    scores = jnp.where(mask, scores, -jnp.inf)
    sink = jnp.broadcast_to(sinks.astype(jnp.float32).reshape(SWA_KV_HEADS, SWA_GROUP, 1, 1, 1),
                            scores.shape[:-1] + (1,))
    probs = jax.nn.softmax(jnp.concatenate([scores, sink], axis=-1), axis=-1)[..., :-1]
    out = jnp.einsum('bhgnqk,bnkhd->bnqhgd', probs.astype(v.dtype), vb)
    return out.reshape(B, S, SWA_QW)

def memory_cross_attention(h, mem, w_q, w_k, w_v, w_o):
    B, S, _ = h.shape
    M = mem.shape[1]
    q = (h @ w_q).reshape(B, S, XA_HEADS, XA_HEAD_DIM)
    k = (mem @ w_k).reshape(B, M, XA_HEADS, XA_HEAD_DIM)
    v = (mem @ w_v).reshape(B, M, XA_HEADS, XA_HEAD_DIM)
    s = jnp.einsum('bqhd,bkhd->bhqk', q, k).astype(jnp.float32) * (XA_HEAD_DIM ** -0.5)
    p = jax.nn.softmax(s, axis=-1).astype(h.dtype)
    o = jnp.einsum('bhqk,bkhd->bqhd', p, v).reshape(B, S, XA_HEADS * XA_HEAD_DIM)
    return o @ w_o

def moe_ffn(h, w_router, b_router, w_gate_up, b_gate_up, w_down, b_down):
    B, S, D = h.shape
    xt = h.reshape(-1, D)
    n = xt.shape[0]
    logits = (xt @ w_router + b_router).astype(jnp.float32)
    top_val, top_idx = lax.top_k(logits, TOP_K)
    gates = jax.nn.softmax(top_val, axis=-1)
    n_assign = n * TOP_K
    e_flat = top_idx.reshape(-1).astype(jnp.int32)
    tok_flat = jnp.repeat(jnp.arange(n, dtype=jnp.int32), TOP_K)
    g_flat = gates.reshape(-1)
    order = jnp.argsort(e_flat)
    e_sorted = e_flat[order]
    counts = jnp.zeros((N_EXPERTS,), jnp.int32).at[e_flat].add(1)
    starts = jnp.cumsum(counts) - counts
    padded = (counts + MOE_BLOCK - 1) // MOE_BLOCK * MOE_BLOCK
    pad_ends = jnp.cumsum(padded)
    pad_starts = pad_ends - padded
    rank = jnp.arange(n_assign, dtype=jnp.int32) - starts[e_sorted]
    dest = pad_starts[e_sorted] + rank
    cap = -(-n_assign // MOE_BLOCK) * MOE_BLOCK + N_EXPERTS * MOE_BLOCK
    n_blocks = cap // MOE_BLOCK
    tok_buf = jnp.zeros((cap,), jnp.int32).at[dest].set(tok_flat[order])
    gate_buf = jnp.zeros((cap,), jnp.float32).at[dest].set(g_flat[order])
    block_start = jnp.arange(n_blocks, dtype=jnp.int32) * MOE_BLOCK
    block_expert = jnp.minimum(jnp.searchsorted(pad_ends, block_start, side='right'), N_EXPERTS - 1)

    def expert_block(args):
        toks, gts, e = args
        xb = xt[toks]
        gu = xb @ w_gate_up[e] + b_gate_up[e]
        x_glu, x_lin = jnp.split(gu, 2, axis=-1)
        x_glu = jnp.minimum(x_glu, SWIGLU_LIMIT)
        x_lin = jnp.clip(x_lin, -SWIGLU_LIMIT, SWIGLU_LIMIT)
        act = x_glu * jax.nn.sigmoid(SWIGLU_ALPHA * x_glu) * (x_lin + 1.0)
        y = act @ w_down[e] + b_down[e]
        return (y.astype(jnp.float32) * gts[:, None])

    y_buf = lax.map(expert_block, (tok_buf.reshape(n_blocks, MOE_BLOCK),
                                   gate_buf.reshape(n_blocks, MOE_BLOCK), block_expert))
    out = jnp.zeros((n, D), jnp.float32).at[tok_buf].add(y_buf.reshape(cap, D))
    return out.astype(h.dtype).reshape(B, S, D)

def setup_inputs(seed: int = 0) -> dict:
    key = jax.random.key(seed)
    ks = jax.random.split(key, 26)
    L, D, E = DEPTH, D_MODEL, N_EXPERTS

    def nrm(k, shape, scale):
        return scale * jax.random.normal(k, shape, jnp.float32)

    return {
        'x': nrm(ks[0], (BATCH, SEQ, D), 1.0),
        'mem': nrm(ks[1], (BATCH, MEM_LEN, D), 1.0),
        't5_table': nrm(ks[2], (T5_BUCKETS, SWA_HEADS), 0.5),
        'lb_logits': nrm(ks[3], (DEPTH + 1, HG_FDIM), 0.5),
        'norm_mix': 1.0 + nrm(ks[4], (L, D), 0.1),
        'w_in': nrm(ks[5], (L, D, IN_COLS), D ** -0.5),
        'b_gates': nrm(ks[6], (L, 2, D), 0.1),
        'hg_norm_gain': 1.0 + nrm(ks[7], (L, HG_DV), 0.1),
        'swa_sinks': nrm(ks[8], (L, SWA_HEADS), 0.5),
        'w_branch_a': nrm(ks[9], (L, HG_VW, D), HG_VW ** -0.5),
        'w_branch_b': nrm(ks[10], (L, SWA_QW, D), SWA_QW ** -0.5),
        'w_mix_out': nrm(ks[11], (L, D, D), D ** -0.5),
        'norm_xa': 1.0 + nrm(ks[12], (L, D), 0.1),
        'xa_w_q': nrm(ks[13], (L, D, XA_HEADS * XA_HEAD_DIM), D ** -0.5),
        'xa_w_k': nrm(ks[14], (L, D, XA_HEADS * XA_HEAD_DIM), D ** -0.5),
        'xa_w_v': nrm(ks[15], (L, D, XA_HEADS * XA_HEAD_DIM), D ** -0.5),
        'xa_w_o': nrm(ks[16], (L, XA_HEADS * XA_HEAD_DIM, D), (XA_HEADS * XA_HEAD_DIM) ** -0.5),
        'norm_ffn': 1.0 + nrm(ks[17], (L, D), 0.1),
        'w_router': nrm(ks[18], (L, D, E), D ** -0.5),
        'b_router': nrm(ks[19], (L, E), 0.01),
        'w_gate_up': nrm(ks[20], (L, E, D, 2 * D_FF), D ** -0.5),
        'b_gate_up': nrm(ks[21], (L, E, 2 * D_FF), 0.02),
        'w_down': nrm(ks[22], (L, E, D_FF, D), D_FF ** -0.5),
        'b_down': nrm(ks[23], (L, E, D), 0.02),
        'norm_final': 1.0 + nrm(ks[24], (D,), 0.1),
    }

def reference(x, mem, t5_table, lb_logits, norm_mix, w_in, b_gates, hg_norm_gain, swa_sinks,
              w_branch_a, w_branch_b, w_mix_out, norm_xa, xa_w_q, xa_w_k, xa_w_v, xa_w_o,
              norm_ffn, w_router, b_router, w_gate_up, b_gate_up, w_down, b_down, norm_final):
    lower_bounds = jnp.cumsum(jax.nn.softmax(lb_logits.astype(jnp.float32), axis=0), axis=0)
    pts = split_points()
    for l in range(DEPTH):
        h = rms_norm(x, norm_mix[l])
        proj = h @ w_in[l]
        hq, hf, hi, hg, sq, sk, sv, ga, gb = jnp.split(proj, pts, axis=-1)
        o_a = hgrn2_mixer(hq, hf, hi, hg, lower_bounds[l], hg_norm_gain[l])
        o_b = swa_mixer(sq, sk, sv, swa_sinks[l], t5_table)
        gate_a = jax.nn.sigmoid(ga + b_gates[l, 0])
        gate_b = jax.nn.sigmoid(gb + b_gates[l, 1])
        merged = gate_a * (o_a @ w_branch_a[l]) + gate_b * (o_b @ w_branch_b[l])
        x = x + merged @ w_mix_out[l]
        x = x + memory_cross_attention(rms_norm(x, norm_xa[l]), mem,
                                       xa_w_q[l], xa_w_k[l], xa_w_v[l], xa_w_o[l])
        x = x + moe_ffn(rms_norm(x, norm_ffn[l]), w_router[l], b_router[l],
                        w_gate_up[l], b_gate_up[l], w_down[l], b_down[l])
    return rms_norm(x, norm_final)


_drawn_inputs = setup_inputs


def setup_inputs(seed=0):
    import zlib

    import numpy as np

    out = dict(_drawn_inputs(seed))
    spreads = {}
    factors = {'swa_sinks': 4.0, 'b_gate_up': 5.343, 'b_down': 6.09}
    for name, (base, spread) in spreads.items():
        noise = np.random.default_rng([zlib.crc32(name.encode()), seed]).standard_normal(out[name].shape)
        drawn = base * np.exp(spread * noise) if base else spread * noise
        out[name] = jnp.asarray(drawn.astype(out[name].dtype))
    for name, factor in factors.items():
        out[name] = (out[name] * factor).astype(out[name].dtype)
    return out
```

```python
import math
from contextlib import ExitStack

import numpy as np

import concourse.bass as bass
from concourse import mybir

P = 128
D = 1024
T = 512
NT = T // P
KD = D // P
MEM = 256
NM = MEM // P
HG_HEADS = 8
HG_PAIRS = HG_HEADS // 2
LEVELS = (64, 32, 16, 8, 4, 2, 1)
SWA_HEADS, SWA_KV, SWA_GROUP, SWA_HD = 16, 4, 4, 64
WINDOW = 128
T5_BUCKETS, T5_EXACT, T5_MAX = 32, 16, 128
XA_HEADS, XA_HD = 4, 256
E = 32
TOPK = 4
FF = 1024
EPS = 1e-5
ALPHA, LIMIT = 1.702, 7.0
NEG = -1e30
COL_Q, COL_F, COL_I, COL_G = 0, 1024, 2048, 3072
COL_SQ, COL_SK, COL_SV, COL_GA, COL_GB = 4096, 5120, 5376, 5632, 6656
MAXB = T * TOPK // P + E
MINB = T * TOPK // P
SKIP = 4096
LINE = 384
SLOT = 2048
RING = 3
M_RAW, M_HI, M_LO = 6, 4, 3
WPB = 12

F32, F32R, BF16 = mybir.dt.float32, mybir.dt.float32r, mybir.dt.bfloat16
I32, I8 = mybir.dt.int32, mybir.dt.int8
ALU = mybir.AluOpType
ACT = mybir.ActivationFunctionType
AX = mybir.AxisListType.X

N_V, N_HG, N_GA, N_SK, N_SV, N_SQ, N_GB, N_MX, N_XK, N_XV, N_XQ, N_WO = 0, 4, 20, 28, 29, 16, 30, 38, 42, 46, 50, 54
N_DENSE = 58


def proj_jobs():
    def pairs(n, name, first):
        return [((name, first + i), 2 * (n % 2) + i) for i in range(2)]
    out = [(("v", c, t), t) for c in range(2) for t in range(NT)]
    for hp in range(HG_PAIRS):
        for s, name in enumerate("fqg"):
            out += pairs(N_HG + 3 * hp + s, name, 2 * hp)
    for j in range(4):
        out += pairs(N_SQ + j, "sq", 2 * j)
    for m in range(4):
        out += pairs(N_GA + 2 * m, "ga", 2 * m) + pairs(N_GA + 2 * m + 1, "wa", 2 * m)
    out += pairs(N_SK, "sk", 0) + pairs(N_SV, "sv", 0)
    out += [(("pv", u), u % 4) for u in range(16)]
    for m in range(4):
        out += pairs(N_GB + 2 * m, "gb", 2 * m) + pairs(N_GB + 2 * m + 1, "wb", 2 * m)
    out += [(("mx", c, t), t) for c in range(2) for t in range(NT)]
    for j in range(4):
        out += pairs(N_XK + j, "xk", 2 * j)
    out += [(("xv", c, m), 2 * c + m) for c in range(2) for m in range(NM)]
    out += pairs(N_XQ, "xq", 0)
    for h in range(XA_HEADS):
        if h + 1 < XA_HEADS:
            out += pairs(N_XQ + h + 1, "xq", 2 * h + 2)
        out += [(("xo", h, c), 2 * (h % 2) + c) for c in range(2)]
    out += [(("wo", c, t), t) for c in range(2) for t in range(NT)]
    out += [(("rt", 0), 0), (("ps", 0), 1), (("cn", 0), 2), (("rl", 0), 3), (("tl", 0), 3)]
    return out


def side_jobs():
    out = [(("T", 0, k), 4 + k % 4) for k in range(KD)]
    for h in range(HG_HEADS):
        out += [(("L", h, i), 4 + i % 2) for i in range(8)]
        out += [(("K", h), 6), (("S", h), 7), (("O", h), 6), (("X", h), 7)]
    for u in range(16):
        out += [(("s", u, e), 4 + e) for e in range(2)] + [(("t", u, e), 6 + e) for e in range(2)]
    out += [(("M", k), 4 + k % 4) for k in range(KD)]
    out += [(("T", 1, k), 4 + k % 4) for k in range(KD)]
    for h in range(XA_HEADS):
        out += [(("xs", h, j), 4 + j) for j in range(2)] + [(("xt", h, j), 6 + j) for j in range(2)]
    out += [(("T", 2, k), 4 + k % 4) for k in range(KD)]
    return out


def t5_bucket_of(dist):
    if dist < T5_EXACT:
        return dist
    f = np.float32
    large = T5_EXACT + int(np.log(f(dist) / f(T5_EXACT)) / f(math.log(T5_MAX / T5_EXACT)) * f(T5_BUCKETS - T5_EXACT))
    return min(large, T5_BUCKETS - 1)


def build(nc, x, mem, t5_table, lb_logits, norm_mix, w_in, b_gates, hg_norm_gain, swa_sinks, w_branch_a,
          w_branch_b, w_mix_out, norm_xa, xa_w_q, xa_w_k, xa_w_v, xa_w_o, norm_ffn, w_router, b_router,
          w_gate_up, b_gate_up, w_down, b_down, norm_final, out):
    ctx = ExitStack()
    ctx.enter_context(nc.allow_non_contiguous_dma(reason="small transposed vectors"))

    base = (nc.sbuf_base + 31) // 32 * 32
    KB = 1024
    RAW, HI, LO = base, base + 24 * KB, base + 48 * KB
    H0 = base + 72 * KB
    O0 = H0 + 32 * KB
    V0 = O0 + 32 * KB
    U0 = V0 + 16 * KB
    S0 = U0 + 32 * KB
    C0 = S0 + 16 * KB

    def at(name, shape, dt, off):
        return nc.alloc_sbuf_tensor_at(name, [P] + list(shape), dt, offset=off)

    raw = [at(f"raw{i}", [SLOT], F32, RAW + i * 8 * KB) for i in range(RING)]
    whi = [at(f"whi{i}", [SLOT], F32R, HI + i * 8 * KB) for i in range(RING)]
    wlo = [at(f"wlo{i}", [SLOT], F32R, LO + i * 8 * KB) for i in range(RING)]
    hT_hi, hT_lo = at("hT_hi", [KD, T], F32R, H0), at("hT_lo", [KD, T], F32R, H0 + 16 * KB)
    o_hi, o_lo = at("o_hi", [KD, T], F32R, O0), at("o_lo", [KD, T], F32R, O0 + 16 * KB)
    xn = at("xn", [NT, D], F32, O0)
    h3g = at("h3g", [NT, D], F32, O0 + 16 * KB)
    x0 = at("x0", [NT, D], F32, V0)
    v_sb = at("v_sb", [NT, D], F32, V0)
    merged = at("merged", [KD, T], F32, V0)
    res = at("res", [NT, D], F32, V0)

    hq = [at(f"hq{i}", [T], F32, U0 + (8 * i + 0) * KB) for i in range(4)]
    hk = [at(f"hk{i}", [T], F32, U0 + (8 * i + 2) * KB) for i in range(4)]
    hG = [at(f"hG{i}", [T], F32, U0 + (8 * i + 4) * KB) for i in range(4)]
    hs = [at(f"hs{i}", [T], F32, U0 + (8 * i + 6) * KB) for i in range(4)]
    lev = [at(f"lev{i}", [T], F32, S0 + 2 * i * KB) for i in range(2)]
    A = at("A", [T], F32, S0 + 4 * KB)
    ON = at("ON", [T], F32, S0 + 6 * KB)
    EG = at("EG", [T], F32, S0 + 8 * KB)
    KDt = at("KDt", [3 * P], F32, S0 + 10 * KB)
    KDT = at("KDT", [3 * P], F32, S0 + 10 * KB + 1536)
    ST = at("ST", [3 * P], F32, S0 + 13 * KB)
    qS = at("qS", [8, T], F32, U0)
    bias = [at("bias0", [8, 256], F32, U0 + 16 * KB), at("bias1", [8, 256], F32, S0 + 8 * KB)]
    Ss = at("Ss", [4, 256], F32, U0 + 24 * KB)
    PTs = [at(f"PTs{e}", [2, 2, P], F32, U0 + (28 + 2 * e) * KB) for e in range(2)]
    kS = at("kS", [2, T], F32, S0)
    vS = at("vS", [NT, 256], F32, S0 + 4 * KB)
    mT_hi, mT_lo = at("mT_hi", [KD, MEM], F32R, U0), at("mT_lo", [KD, MEM], F32R, U0 + 8 * KB)
    memr = at("memr", [NM, D], F32, U0 + 16 * KB)
    qx = [at(f"qx{i}", [2, T], F32, U0 + (16 + 4 * i) * KB) for i in range(2)]
    Px = [at(f"Px{i}", [2, MEM], F32, U0 + (24 + 2 * i) * KB) for i in range(2)]
    PTx = at("PTx", [NM, NT, P], F32, U0 + 28 * KB)
    kx = at("kx", [KD, MEM], F32, S0)
    vx = at("vx", [NM, D], F32, S0 + 8 * KB)
    xg = at("xg", [D], F32, H0)
    xgT_hi, xgT_lo = at("xgT_hi", [KD, P], F32R, H0 + 4 * KB), at("xgT_lo", [KD, P], F32R, H0 + 8 * KB)
    act = at("act", [FF], F32, H0 + 12 * KB)
    glu = at("glu", [FF], F32, H0 + 16 * KB)
    sig = at("sig", [FF], F32, H0 + 20 * KB)
    aT_hi, aT_lo = at("aT_hi", [KD, P], F32R, H0 + 24 * KB), at("aT_lo", [KD, P], F32R, H0 + 28 * KB)
    ysb = at("ysb", [D], F32, O0)
    m_raw_at = raw + [at(f"raw{RING + i}", [SLOT], F32, O0 + 8 * (i + 1) * KB) for i in range(M_RAW - RING)]
    m_hi_at = whi + [at(f"whi{RING}", [SLOT], F32R, U0)]
    m_lo_at = wlo
    biasf = at("biasf", [3 * D], F32, U0)
    biasS = at("biasS", [3 * D], BF16, U0 + 12 * KB)
    r0 = U0 + 18 * KB
    gbc = at("gbc", [D], F32, r0)
    small = [r0 + 4 * KB]

    def sm(name, shape, dt=F32, where=small):
        n = int(np.prod(shape)) * {F32: 4, F32R: 4, I32: 4, BF16: 2, I8: 1}[dt]
        off = where[0]
        where[0] = off + (n + 31) // 32 * 32
        return at(name, shape, dt, off)

    wr = sm("wr", [KD, E]); wr_hi = sm("wr_hi", [KD, E], F32R); wr_lo = sm("wr_lo", [KD, E], F32R)
    br = sm("br", [E]); lg = sm("lg", [NT, E]); v8 = sm("v8", [NT, 8])
    gt = sm("gt", [NT, E]); eq = sm("eq", [NT, E]); cs = sm("cs", [NT, E]); need = sm("need", [NT])
    ch = sm("ch", [NT, E]); ex = sm("ex", [NT, E]); den = sm("den", [NT])
    assert small[0] <= S0
    small[0] = S0
    chb = sm("chb", [NT, E], BF16); pos = sm("pos", [NT, E]); cnt = sm("cnt", [E]); nbe = sm("nbe", [E])
    bend = sm("bend", [E]); bst = sm("bst", [E]); bq = sm("bq", [NT, E]); oh = sm("oh", [NT, E])
    tmp4 = sm("tmp4", [NT, E]); BL = sm("BL", [NT, TOPK]); JJ = sm("JJ", [NT, TOPK]); GT = sm("GT", [NT, TOPK])
    tokid4 = sm("tokid4", [NT, TOPK])
    iob = sm("iob", [MAXB]); ioj = sm("ioj", [P]); tokid = sm("tokid", [NT])
    ohj = [sm(f"ohj{i}", [P]) for i in range(2)]; ohb = [sm(f"ohb{i}", [2, MAXB]) for i in range(2)]
    lists = sm("lists", [2, MAXB]); empty = sm("empty", [2, MAXB]); lists_i = sm("lists_i", [2, MAXB], I32); bex = sm("bex", [MAXB]); bex_i = sm("bex_i", [MAXB], I32)
    nb_i = sm("nb_i", [1], I32); pm = sm("pm", [1]); selb = sm("selb", [MAXB], BF16)
    selt = sm("selt", [P], BF16); idx = sm("idx", [1], I32); idy = sm("idy", [1], I32); U_lt = sm("U_lt", [P], BF16)
    ones_b = sm("ones_b", [P], BF16)
    big = sm("big", [MAXB, E])
    lgT = sm("lgT", [T])
    assert small[0] <= C0, (small[0] - S0)
    yg = [at(f"yg{i}", [D], F32, H0 + 4 * i * KB) for i in range(8)]
    fin = at("fin", [NT, D], F32, O0)
    gfin = at("gfin", [D], F32, O0 + 16 * KB)

    cc = [C0]

    def co(name, shape, dt=F32):
        return sm(name, shape, dt, cc)
    ident = co("ident", [P]); scan1 = co("scan1", [T])
    lmask = co("lmask", [7, 256], I8)
    gain = [co(f"gain{i}", [KD]) for i in range(3)]
    hgain = co("hgain", [1]); lbl = co("lbl", [2, KD]); lb = co("lb", [KD]); oml = co("oml", [KD])
    lbt = co("lbt", [KD]); bgt = co("bgt", [2, KD]); sinks = co("sinks", [SWA_HEADS])
    ss = co("ss", [NT]); rs = co("rs", [NT]); mhalf = co("mhalf", [NT]); dec = co("dec", [NT])
    gmark = co("gmark", [2]); mx = co("mx", [4]); mn = co("mn", [4]); es = co("es", [4]); dn = co("dn", [4]); rd = co("rd", [4])
    line = at("line", [LINE], F32, S0); t5T = at("t5T", [T5_BUCKETS], F32, S0 + 2 * KB)
    GATE = [at(f"gate{i}", [T], F32, S0 + (8 + 2 * i) * KB) for i in range(2)]
    assert cc[0] <= nc.sbuf_usable_end, cc[0] - nc.sbuf_usable_end

    ps = [ctx.enter_context(nc.psum_tensor(f"bank{i}", [P, 512], F32)) for i in range(8)]

    line_d = nc.dram_tensor("line_d", [SWA_HEADS, LINE], F32, kind="Internal").ap()
    lines_d = nc.dram_tensor("lines_d", [P, SWA_HEADS * LINE], F32, kind="Internal").ap()
    h3_d = nc.dram_tensor("h3_d", [T, D], F32, kind="Internal").ap()
    y_d = nc.dram_tensor("y_d", [T * TOPK, D], F32, kind="Internal").ap()

    def sem(name):
        return ctx.enter_context(nc.semaphore(name))
    raw_in = [sem(f"raw_in{i}") for i in range(RING)]
    hi_done = [sem(f"hi_done{i}") for i in range(RING)]
    lo_done = [sem(f"lo_done{i}") for i in range(RING)]
    w_used = sem("w_used")
    bank_full = [sem(f"bank_full{i}") for i in range(8)]
    bank_free = [sem(f"bank_free{i}") for i in range(8)]
    act_step, dve_step, pool_step = sem("act_step"), sem("dve_step"), sem("pool_step")
    x_in = [sem(f"x_in{t}") for t in range(NT)]
    const_in, line_in, mem_in, line_out, bias_in = sem("const_in"), sem("line_in"), sem("mem_in"), sem("line_out"), sem("bias_in")
    res_in, rt_in, h3_out, bf_in = sem("res_in"), sem("rt_in"), sem("h3_out"), sem("bf_in")
    pool_const = sem("pool_const")
    gain_in = sem("gain_in")
    sumsq, rstd, xn_ready, hT_hi_ready, hT_ready = sem("sumsq"), sem("rstd"), sem("xn_ready"), sem("hT_hi_ready"), sem("hT_ready")
    v_ready = sem("v_ready")
    f_sig, f_gate, log_f = sem("f_sig"), sem("f_gate"), sem("log_f")
    q_sig, q_ready, g_sig, g_ready = sem("q_sig"), sem("q_ready"), sem("g_sig"), sem("g_ready")
    G_ready, lev_diff, lev_exp, lev_ready = sem("G_ready"), sem("lev_diff"), sem("lev_exp"), sem("lev_ready")
    eg_ready, dec_ready, qe_ready = sem("eg_ready"), sem("dec_ready"), sem("qe_ready")
    kd_diff, kd_exp, kd_ready, kdt_ready, st_ready, A_ready = (sem("kd_diff"), sem("kd_exp"), sem("kd_ready"),
                                                               sem("kdt_ready"), sem("st_ready"), sem("A_ready"))
    o_sq, o_ss, o_rs, on_ready, ob_ready, o_hi_ready, o_ready = (sem("o_sq"), sem("o_ss"), sem("o_rs"), sem("on_ready"),
                                                                 sem("ob_ready"), sem("o_hi_ready"), sem("o_ready"))
    merged_b = sem("merged_b")
    qS_ready, kS_ready, vS_ready = sem("qS_ready"), sem("kS_ready"), sem("vS_ready")
    s_max, s_exp, s_norm, pt_ready, ob_hi = sem("s_max"), sem("s_exp"), sem("s_norm"), sem("pt_ready"), sem("ob_hi")
    m_hi, m_ready, mg_hi, mg_ready = sem("m_hi"), sem("m_ready"), sem("mg_hi"), sem("mg_ready")
    xg_clear, idy_ready = sem("xg_clear"), sem("idy_ready")
    lines_out, fin_in, list_mm = sem("lines_out"), sem("fin_in"), sem("list_mm")
    kx_ready, vx_ready, qx_ready = sem("kx_ready"), sem("vx_ready"), sem("qx_ready")
    xs_max, xs_exp, xs_norm, ptx_ready, xo_hi, xo_ready = (sem("xs_max"), sem("xs_exp"), sem("xs_norm"),
                                                           sem("ptx_ready"), sem("xo_hi"), sem("xo_ready"))
    h3g_ready, wr_hi_s, wr_ready, ex_in, ex_out = sem("h3g_ready"), sem("wr_hi_s"), sem("wr_ready"), sem("ex_in"), sem("ex_out")
    ch_ready, onehot, list_ready, biasS_ready, disp_const = (sem("ch_ready"), sem("onehot"), sem("list_ready"),
                                                             sem("biasS_ready"), sem("disp_const"))
    m_raw = [sem(f"m_raw{i}") for i in range(M_RAW)]
    m_hid = sem("m_hid")
    m_lod_v, m_lod_p = sem("m_lod_v"), sem("m_lod_p")
    m_used = sem("m_used")
    idx_ready, xg_in, xgT_full, xgT_hi_r, xgT_ready = sem("idx_ready"), sem("xg_in"), sem("xgT_full"), sem("xgT_hi_r"), sem("xgT_ready")
    sel_ready, gmin, gsig, act_ready, aT_full, aT_hi_r, aT_ready = (sem("sel_ready"), sem("gmin"), sem("gsig"), sem("act_ready"),
                                                                    sem("aT_full"), sem("aT_hi_r"), sem("aT_ready"))
    glu_free, y_copied, y_out = sem("glu_free"), sem("y_copied"), sem("y_out")
    blocks_done = sem("blocks_done")
    m_chain = sem("m_chain")
    yg_in = [sem(f"yg_in{i}") for i in range(8)]
    yg_used, fin_sq, fin_rs, fin_ready, out_done = sem("yg_used"), sem("fin_sq"), sem("fin_rs"), sem("fin_ready"), sem("out_done")

    ordinal, bank_of, seen = {}, {}, [0] * 8
    for key, b in proj_jobs() + side_jobs():
        ordinal[key], bank_of[key] = seen[b], b
        seen[b] += 1

    def full(eng, key):
        eng.wait_ge(bank_full[bank_of[key]], full_at[key])

    full_at, fcount = {}, [0] * 8
    for key, b in proj_jobs() + side_jobs():
        if b >= 4 or key[0] in ("pv", "xo", "rt", "rl", "ps", "cn", "tl"):
            fcount[b] += 1
            full_at[key] = fcount[b]

    def opened(eng, key):
        if ordinal[key]:
            eng.wait_ge(bank_free[bank_of[key]], ordinal[key])

    def free(ins, key):
        ins.then_inc(bank_free[bank_of[key]], 1)

    def was_freed(eng, key):
        eng.wait_ge(bank_free[bank_of[key]], ordinal[key] + 1)

    def used(eng, n):
        eng.wait_ge(w_used, n + 1)

    class Chain:
        def __init__(self):
            self.n = {}

        def inc(self, ins, s):
            ins.then_inc(s, 1)
            self.n[id(s)] = self.n.get(id(s), 0) + 1

        def last(self, eng, s):
            eng.wait_ge(s, self.n[id(s)])

    W = w_in[0]

    def cols_slot(w, c0, n=256):
        return w.rearrange("(k p) c -> p k c", p=P)[:, :, c0:c0 + n]

    def half_slot(w, c, kh):
        return w.rearrange("(k p) c -> p k c", p=P)[:, 4 * kh:4 * kh + 4, 512 * c:512 * c + 512]

    def slot_loads(n, dst):
        v8x = dst.rearrange("p (k c) -> p k c", c=256)
        v4x = dst.rearrange("p (k c) -> p k c", c=512)
        if n < N_HG:
            c, kh = n // 2, n % 2
            return [(v4x, W.rearrange("(k p) c -> p k c", p=P)[:, 4 * kh:4 * kh + 4, COL_I + 512 * c:COL_I + 512 * c + 512])]
        if n < N_SQ:
            hp, s = divmod(n - N_HG, 3)
            return [(v8x, cols_slot(W, (COL_F, COL_Q, COL_G)[s] + 256 * hp))]
        if n < N_GA:
            p_, gh = divmod(n - N_SQ, 2)
            return [(v8x[:, :, 128 * i + 64 * e:128 * i + 64 * e + 64],
                     cols_slot(W, COL_SQ + (8 * p_ + 4 * e + 2 * gh + i) * SWA_HD, SWA_HD))
                    for i in range(2) for e in range(2)]
        if n < N_SK:
            m, s = divmod(n - N_GA, 2)
            return [(v8x, cols_slot(w_branch_a[0], 256 * m) if s else cols_slot(W, COL_GA + 256 * m))]
        if n < N_GB:
            return [(v8x, cols_slot(W, (COL_SK, COL_SV)[n - N_SK]))]
        if n < N_MX:
            m, s = divmod(n - N_GB, 2)
            if not s:
                return [(v8x, cols_slot(W, COL_GB + 256 * m))]
            wb = w_branch_b[0].rearrange("(a e g i) c -> a e i g c", a=2, e=2, g=4)
            return [(v8x[64 * e:64 * e + 64, 4 * a:4 * a + 4, :], wb[a, e][:, :, 256 * m:256 * m + 256])
                    for a in range(2) for e in range(2)]
        if n < N_XK:
            return [(v4x, half_slot(w_mix_out[0], *divmod(n - N_MX, 2)))]
        if n < N_XV:
            return [(v8x, cols_slot(xa_w_k[0], 256 * (n - N_XK)))]
        if n < N_XQ:
            return [(v4x, half_slot(xa_w_v[0], *divmod(n - N_XV, 2)))]
        if n < N_WO:
            return [(v8x, cols_slot(xa_w_q[0], 256 * (n - N_XQ)))]
        return [(v4x, half_slot(xa_w_o[0], *divmod(n - N_WO, 2)))]

    raw_at, so_far = [], [0] * RING
    for n in range(N_DENSE):
        so_far[n % RING] += 16 * len(slot_loads(n, raw[0][:]))
        raw_at.append(so_far[n % RING])

    def h2(tile_, k, t):
        return tile_[:, k, t * P:(t + 1) * P]

    POOL_LO = (5, 9)

    def m_low(eng, k, j):
        if j in POOL_LO:
            eng.wait_ge(m_lod_p, k * len(POOL_LO) + POOL_LO.index(j) + 1 + len(POOL_LO))
        else:
            own = [i for i in range(WPB) if i not in POOL_LO]
            eng.wait_ge(m_lod_v, k * len(own) + own.index(j) + 1 + len(own))

    def m_low_before(eng, k, j):
        i = (j - M_RAW) % WPB
        if j >= M_RAW:
            m_low(eng, k, i)
        elif i in POOL_LO:
            eng.wait_ge(m_lod_p, k * len(POOL_LO) + POOL_LO.index(i) + 1)
        else:
            own = [x for x in range(WPB) if x not in POOL_LO]
            eng.wait_ge(m_lod_v, k * len(own) + own.index(i) + 1)

    def make_low(eng, ops, k, j):
        eng.wait_ge(m_hid, k * WPB + j + 1)
        eng.wait_ge(m_used, k * WPB + j + 1 + M_HI - M_LO)
        ops.tensor_tensor(m_lo_at[j % M_LO][:], m_raw_at[j % M_RAW][:], m_hi_at[j % M_HI][:].bitcast(F32),
                          ALU.subtract).then_inc(m_lod_p if j in POOL_LO else m_lod_v, 1)

    block = ctx.enter_context(nc.Block())

    @block.sync
    def _(sp):
        xt = x[0].rearrange("(t p) d -> t p d", p=P)
        for t in range(NT):
            sp.dma_start(x0[:, t, :], xt[t]).then_inc(x_in[t], 16)
        for n in range(N_DENSE):
            if n >= RING:
                sp.wait_ge(lo_done[n % RING], n // RING)
            for dst, src in slot_loads(n, raw[n % RING][:]):
                sp.dma_start(dst, src).then_inc(raw_in[n % RING], 16)
            if n == RING:
                sp.wait_ge(line_in, 1)
                sp.dma_start(line_d, line[0:SWA_HEADS, :]).then_inc(line_out, 16)
            if n == 2 * RING:
                sp.wait_ge(line_out, 16)
                sp.dma_start(lines_d, bass.AP(line_d.tensor, 0, [[0, P], [1, SWA_HEADS * LINE]])).then_inc(lines_out, 16)
            if n == N_SK + 2:
                sp.wait_ge(lines_out, 16)
                was_freed(sp, ("wa", 7))
                was_freed(sp, ("wa", 6))
                for p_ in range(2):
                    src = bass.AP(lines_d.tensor, (8 * p_) * LINE + P - 1,
                                  [[SWA_HEADS * LINE - 1, P], [LINE, 8], [1, 256]])
                    sp.dma_start(bias[p_][:], src).then_inc(bias_in, 16)
            if n == N_GB + 2:
                sp.wait_ge(s_max, 16)
                sp.dma_start(memr[:], mem[0].rearrange("(m p) d -> p m d", p=P)).then_inc(mem_in, 16)
            if n == N_MX + 2:
                sp.wait_ge(mg_ready, KD)
                sp.dma_start(res[:], x[0].rearrange("(t p) d -> p t d", p=P)).then_inc(res_in, 16)
        hd = h3_d.rearrange("(t p) d -> t p d", p=P)
        for t in range(NT):
            sp.wait_ge(h3g_ready, t + 1)
            sp.dma_start(hd[t], h3g[:, t, :]).then_inc(h3_out, 16)
        def expert_slots(e, k, js):
            gu = w_gate_up[0][e].rearrange("a (k p) c -> p (a k) c", p=P)
            dn_ = w_down[0][e].rearrange("a (k p) c -> p (a k) c", p=P)
            for j in js:
                if k is not None:
                    m_low_before(sp, k, j)
                if j < 8:
                    c, kh = divmod(j, 2)
                    col = (c % 2) * FF + (c // 2) * 512
                    src = gu[:, 4 * kh:4 * kh + 4, col:col + 512]
                else:
                    kh, oc = divmod(j - 8, 2)
                    src = dn_[:, 4 * kh:4 * kh + 4, oc * 512:oc * 512 + 512]
                sp.dma_start(m_raw_at[j % M_RAW][:].rearrange("p (k c) -> p k c", c=512), src).then_inc(m_raw[j % M_RAW], 16)
        for j in range(RING):
            sp.wait_ge(lo_done[j], (N_DENSE - 1 - j) // RING + 1)
            expert_slots(slice(0, 1), None, [j])
        sp.wait_ge(h3_out, 16 * NT)
        expert_slots(slice(0, 1), None, range(RING, M_RAW))
        sp.wait_ge(list_ready, 1)
        nb = sp.value_load(nb_i[0:1, 0:1], min_val=MINB, max_val=MAXB - 1)
        with sp.Fori(0, nb - 1) as k:
            e = sp.value_load(bex_i[0:1, bass.ds(k, 1)], min_val=0, max_val=E - 1)
            expert_slots(bass.ds(e, 1), k, range(M_RAW, WPB))
            e2 = sp.value_load(bex_i[0:1, bass.ds(k + 1, 1)], min_val=0, max_val=E - 1)
            expert_slots(bass.ds(e2, 1), k + 1, range(M_RAW))
        e = sp.value_load(bex_i[0:1, bass.ds(nb - 1, 1)], min_val=0, max_val=E - 1)
        expert_slots(bass.ds(e, 1), nb - 1, range(M_RAW, WPB))
        sp.wait_ge(blocks_done, 1)
        yv = y_d.rearrange("(t p r) d -> t r p d", p=P, r=TOPK)
        for i in range(NT * TOPK):
            if i >= 8:
                sp.wait_ge(yg_used, i - 7)
            sp.dma_start(yg[i % 8][:], yv[i // TOPK, i % TOPK]).then_inc(yg_in[i % 8], 16)
        ot = out[0].rearrange("(t p) d -> t p d", p=P)
        for t in range(NT):
            sp.wait_ge(fin_ready, t + 1)
            sp.dma_start(ot[t], fin[:, t, :]).then_inc(out_done, 16)
        sp.wait_ge(out_done, 16 * NT)
        sp.wait_ge(h3_out, 16 * NT)
        sp.wait_ge(line_out, 16)
        sp.wait_ge(lines_out, 16)

    @block.gpsimd
    def _(pool):
        g = nc.gpsimd
        ck = Chain()

        def step(ins):
            ck.inc(ins, pool_step)
            ck.last(pool, pool_step)
        step(g.memset(ident[:], 0.0))
        step(g.affine_select(out=ident[:], in_=ident[:], compare_op=ALU.not_equal, fill=1.0, base=0,
                             pattern=[[-1, P]], channel_multiplier=1))
        step(g.memset(mhalf[:], -0.5))
        ck.inc(g.memset(line[0:SWA_HEADS, :], NEG), pool_const)
        def rstd_of(src, i, n, s, scale):
            step(g.tensor_scalar(rs[:, i:i + n], src, scale, EPS, ALU.mult, ALU.add))
            g.tensor_tensor(rs[:, i:i + n], rs[:, i:i + n], mhalf[:, i:i + n], ALU.pow).then_inc(s, 1)

        def norm(stage):
            for t in range(NT):
                pool.wait_ge(sumsq, NT * stage + t + 1)
                if stage:
                    pool.wait_ge(xn_ready, NT * (stage - 1) + t + 1)
                rstd_of(ss[:, t:t + 1], t, 1, rstd, 1.0 / D)
        norm(0)
        step(g.memset(scan1[:], 1.0))
        step(g.memset(scan1[:].rearrange("p (c t) -> p c t", t=P)[:, :, 0:1], 0.0))
        step(g.memset(gmark[:], 0.0))
        step(g.memset(lmask[:], 1.0))
        for i, c in enumerate(LEVELS):
            nblk = P // (2 * c)
            m = lmask[:, i, :].rearrange("p (a b c) -> p a b c", a=4, b=nblk)
            step(g.affine_select(out=m, in_=m, compare_op=ALU.is_ge, fill=0.0, base=0,
                                 pattern=[[0, 4], [-2 * c, nblk], [0, c]], channel_multiplier=1))
            step(g.affine_select(out=m, in_=m, compare_op=ALU.is_ge, fill=0.0, base=c - 1,
                                 pattern=[[0, 4], [2 * c, nblk], [0, c]], channel_multiplier=-1))
        pool.sem_inc(pool_const, 1)

        def hgrn(hp):
            for h in (2 * hp, 2 * hp + 1):
                b = h % 4
                G = hG[b]
                pool.wait_ge(G_ready, h + 1)
                for i, c in enumerate(LEVELS):
                    n = 7 * h + i
                    L = lev[n % 2]
                    if n >= 2:
                        ph, pi = divmod(n - 2, 7)
                        full(pool, ("L", ph, pi + 1))
                    Gv = G[:].rearrange("p (b c) -> p b c", c=2 * c)
                    Lv = L[:].rearrange("p (b c) -> p b c", c=2 * c)
                    ref = Gv[:, :, c - 1:c].to_broadcast([P, T // (2 * c), c])
                    g.tensor_tensor(Lv[:, :, 0:c], ref, Gv[:, :, 0:c], ALU.subtract)
                    g.tensor_tensor(Lv[:, :, c:2 * c], Gv[:, :, c:2 * c], ref, ALU.subtract).then_inc(lev_diff, 1)
                    if i == 0:
                        G3 = G[:].rearrange("p (c t) -> p c t", t=P)[:, 0:3, :]
                        if h:
                            full(pool, ("K", h - 1))
                        last = G3[:, :, P - 1:P].to_broadcast([P, 3, P])
                        g.tensor_tensor(KDt[:].rearrange("p (c t) -> p c t", t=P), last, G3, ALU.subtract).then_inc(kd_diff, 1)
                        pool.wait_ge(kd_exp, h + 1)
                        g.tensor_tensor(KDt[:], KDt[:], hk[b][:, 0:3 * P], ALU.mult).then_inc(kd_ready, 1)
                    if i == 3:
                        pool.wait_ge(dec_ready, h + 1)
                        g.tensor_tensor(EG[:], EG[:], hq[b][:], ALU.mult).then_inc(qe_ready, 1)
                pool.wait_ge(o_ss, h + 1)
                rstd_of(ss[:, 0:NT], 0, NT, o_rs, 1.0 / P)
        for hp in range(HG_PAIRS):
            hgrn(hp)
        norm(1)
        for h in (2, 3):
            for c in range(2):
                was_freed(pool, ("xo", h, c))
        step(g.iota(iob[:], pattern=[[1, MAXB]], base=0, channel_multiplier=0, allow_small_or_imprecise_dtypes=True))
        step(g.iota(ioj[:], pattern=[[1, P]], base=0, channel_multiplier=0, allow_small_or_imprecise_dtypes=True))
        step(g.iota(tokid[:], pattern=[[P, NT]], base=1, channel_multiplier=1, allow_small_or_imprecise_dtypes=True))
        step(g.iota(tokid4[:], pattern=[[P * TOPK, NT], [1, TOPK]], base=1, channel_multiplier=TOPK,
                    allow_small_or_imprecise_dtypes=True))
        for q in range(3):
            step(g.iota(pm[32 * q:32 * q + 32, :], pattern=[[0, 1]], base=0, channel_multiplier=1,
                        allow_small_or_imprecise_dtypes=True))
        step(g.memset(ones_b[:], 1.0))
        g.affine_select(out=U_lt[:], in_=ones_b[:], compare_op=ALU.is_gt, fill=0.0, base=0,
                        pattern=[[1, P]], channel_multiplier=-1).then_inc(disp_const, 1)
        norm(2)
        pool.wait_ge(bf_in, 96)

        def cast(a, b):
            step(g.tensor_copy(biasS[a:b, :], biasf[a:b, :]))

        def rest(a, b):
            step(g.tensor_tensor(biasf[a:b, :], biasf[a:b, :], biasS[a:b, :], ALU.subtract))
        cast(0, 96); rest(0, 64); cast(0, 64); rest(0, 32)
        g.tensor_copy(biasS[0:32, :], biasf[0:32, :]).then_inc(biasS_ready, 1)

        pool.wait_ge(list_ready, 1)
        pool.wait_ge(h3_out, 16 * NT)
        nb = pool.value_load(nb_i[0:1, 0:1], min_val=MINB, max_val=MAXB - 1)

        def gather():
            g.indirect_dma_start(xg[:], None, h3_d, bass.IndirectOffsetOnAxis(ap=idx[:, 0:1], axis=0),
                                 bounds_check=T - 1, oob_is_err=False).then_inc(xg_in, 16)
        def scatter():
            g.indirect_dma_start(y_d, bass.IndirectOffsetOnAxis(ap=idy[:, 0:1], axis=0), ysb[:], None,
                                 bounds_check=T * TOPK - 1, oob_is_err=False).then_inc(y_out, 16)
        pool.wait_ge(idx_ready, 1)
        pool.wait_ge(xg_clear, 1)
        gather()
        own = len(POOL_LO)
        pool.sem_inc(m_lod_p, own)
        with pool.Fori(0, nb) as k:
            pool.wait_ge(idx_ready, k + 2)
            pool.wait_ge(xgT_full, k * 2 + 2)
            g.tensor_tensor(gmark[:, 0:1], gmark[:, 0:1], gmark[:, 0:1], ALU.add)
            gather()
            pool.wait_ge(idy_ready, k + 1)
            pool.wait_ge(y_copied, k * 2 + 2)
            g.tensor_tensor(gmark[:, 1:2], gmark[:, 1:2], gmark[:, 1:2], ALU.add)
            scatter()
            for j in POOL_LO:
                make_low(pool, g, k, j)
        pool.wait_ge(idy_ready, nb + 1)
        pool.wait_ge(y_copied, nb * 2 + 2)
        g.tensor_tensor(gmark[:, 1:2], gmark[:, 1:2], gmark[:, 1:2], ALU.add)
        scatter()
        for t in range(NT):
            pool.wait_ge(fin_sq, t + 1)
            rstd_of(ss[:, t:t + 1], t, 1, fin_rs, 1.0 / D)

    @block.scalar
    def _(act_):
        s = nc.scalar
        ck = Chain()

        def vec(dst, src, sm_=const_in):
            act_.dma_start(dst, src).then_inc(sm_, 16)
        vec(gain[0][:], norm_mix[0].rearrange("(k p) -> p k", p=P), gain_in)
        vec(gain[1][:], norm_xa[0].rearrange("(k p) -> p k", p=P))
        vec(gain[2][:], norm_ffn[0].rearrange("(k p) -> p k", p=P))
        vec(hgain[:], hg_norm_gain[0].rearrange("(p a) -> p a", a=1))
        for i in range(2):
            vec(lbl[:, i, :], lb_logits[i].rearrange("(k p) -> p k", p=P))
            vec(bgt[:, i, :], b_gates[0, i].rearrange("(k p) -> p k", p=P))
        vec(sinks[:], bass.AP(swa_sinks.tensor, 0, [[0, P], [1, SWA_HEADS]]))
        vec(t5T[0:SWA_HEADS, :], t5_table.rearrange("b h -> h b"))
        CONSTS = 16 * 9

        nxt = [0]

        def split_to(n):
            while nxt[0] <= min(n, N_DENSE - 1):
                m = nxt[0]
                nxt[0] += 1
                act_.wait_ge(raw_in[m % RING], raw_at[m])
                if m >= RING:
                    used(act_, m - RING)
                s.activation(whi[m % RING][:], raw[m % RING][:], ACT.Copy).then_inc(hi_done[m % RING], 1)

        def norm(stage, src, wait_src):
            for t in range(NT):
                wait_src(t)
                s.activation(xn[:, t, :], src[:, t, :], ACT.Square, accum_out=ss[:, t:t + 1]).then_inc(sumsq, 1)

        def to_hT(stage):
            for k in range(KD):
                full(act_, ("T", stage, k))
                s.activation(hT_hi[:, k, :], ps[bank_of[("T", stage, k)]][:], ACT.Copy,
                             scale=gain[stage][:, k:k + 1]).then_inc(hT_hi_ready, 1)

        norm(0, x0, lambda t: act_.wait_ge(x_in[t], 16))
        split_to(1)
        act_.wait_ge(gain_in, 16)
        to_hT(0)
        act_.wait_ge(const_in, CONSTS)
        act_.wait_ge(dve_step, 3)
        s.activation(lbl[:], lbl[:], ACT.Exp).then_inc(act_step, 1)
        for c in range(2):
            split_to(N_V + 2 * c + 3)
            used(act_, N_V + 2 * c + 1)
            for t in range(NT):
                ins = s.activation(v_sb[:, t, 512 * c:512 * c + 512], ps[t][:], ACT.Copy)
                free(ins, ("v", c, t))

        def hgrn(hp):
            for h in (2 * hp, 2 * hp + 1):
                b = h % 4
                yield
                for i in range(7):
                    n = 7 * h + i
                    act_.wait_ge(lev_diff, n + 1)
                    s.activation(lev[n % 2][:], lev[n % 2][:], ACT.Exp).then_inc(lev_exp, 1)
                    if i == 0:
                        act_.wait_ge(kd_diff, h + 1)
                        s.activation(KDt[:], KDt[:], ACT.Exp).then_inc(kd_exp, 1)
                        if h:
                            full(act_, ("O", h - 1))
                        s.activation(EG[:], hG[b][:], ACT.Exp).then_inc(eg_ready, 1)
                    yield
                    if i == 0:
                        full(act_, ("K", h))
                        ins = s.activation(KDT[:], ps[6][:, 0:3 * P], ACT.Copy)
                        free(ins, ("K", h))
                        yield
                        if h % 2:
                            yield from x_part(h - 1)
                    if i == 2:
                        yield
                full(act_, ("O", h))
                if h:
                    act_.wait_ge(o_ready, h)
                s.activation(ON[:], ps[6][:], ACT.Square).then_inc(o_sq, 1)
                yield
            yield from x_part(2 * hp + 1)

        def x_part(h):
            was_freed(act_, ("X", h))
            s.activation(o_hi[:, h, :], ON[:], ACT.Copy).then_inc(o_hi_ready, 1)
            yield

        def advance(gen, n):
            for _ in range(n):
                next(gen, None)

        filler = iter(())
        for hp in range(HG_PAIRS):
            n0 = N_HG + 3 * hp
            b0 = (2 * hp) % 4
            advance(filler, 8)
            split_to(n0 + 2)
            used(act_, n0)
            for i in range(2):
                h = 2 * hp + i
                bank = ps[bank_of[("f", h)]]
                s.activation(hG[b0 + i][:], bank[:], ACT.Sigmoid).then_inc(act_step, 1)
                free(s.activation(hk[b0 + i][:], bank[:], ACT.Sigmoid, scale=-1.0), ("f", h))
            advance(filler, 8)
            split_to(n0 + 3)
            used(act_, n0 + 1)
            for i in range(2):
                s.activation(hq[b0 + i][:], ps[bank_of[("q", 2 * hp + i)]][:], ACT.Sigmoid).then_inc(q_sig, 1)
            advance(filler, 8)
            split_to(n0 + 4)
            used(act_, n0 + 2)
            for i in range(2):
                s.activation(hs[b0 + i][:], ps[bank_of[("g", 2 * hp + i)]][:], ACT.Sigmoid).then_inc(g_sig, 1)
            for i in range(2):
                act_.wait_ge(f_gate, 2 * hp + i + 1)
                s.activation(hG[b0 + i][:], hG[b0 + i][:], ACT.Ln).then_inc(log_f, 1)
            advance(filler, 99)
            filler = hgrn(hp)
        for j in range(4):
            advance(filler, 6)
            split_to(N_SQ + j + 2)
            used(act_, N_SQ + j)
            if j == 0:
                act_.wait_ge(o_ready, HG_HEADS - 2)
            for i in range(2):
                free(s.activation(qS[:, 2 * j + i, :], ps[bank_of[("sq", 2 * j + i)]][:], ACT.Copy), ("sq", 2 * j + i))
        advance(filler, 99)
        split_to(N_GA + 2)

        def gates(n0, ga, which):
            for m in range(4):
                split_to(n0 + 2 * m + 2)
                used(act_, n0 + 2 * m)
                for i in range(2):
                    k = 2 * m + i
                    n = 8 * which + k
                    if n >= 2:
                        if which and k >= 2:
                            act_.wait_ge(merged_b, k - 1)
                        else:
                            was_freed(act_, ("wa", (n - 2) % 8))
                    free(s.activation(gate_t[n % 2][:], ps[bank_of[(ga, k)]][:], ACT.Sigmoid,
                                      bias=bgt[:, which, k:k + 1]), (ga, k))
                split_to(n0 + 2 * m + 3)
        gate_t = GATE
        gates(N_GA, "ga", 0)

        split_to(N_SK + 2)
        used(act_, N_SK)
        act_.wait_ge(o_ready, HG_HEADS)
        for i in range(2):
            free(s.activation(kS[:, i, :], ps[bank_of[("sk", i)]][:], ACT.Copy), ("sk", i))
        split_to(N_SK + 3)
        used(act_, N_SV)
        for i in range(2):
            free(s.activation(vS[:, 2 * i:2 * i + 2, :], ps[bank_of[("sv", i)]][:].rearrange("p (t c) -> p t c", t=2),
                              ACT.Copy), ("sv", i))
        split_to(N_GB + 2)
        for u in range(17):
            if u < 16:
                p_, gh, n = u // 8, (u // 4) % 2, u % 4
                w0 = P if n == 0 else 0
                act_.wait_ge(s_max, u + 1)
                for j in range(4):
                    s.activation(Ss[:, j, w0:256], Ss[:, j, w0:256], ACT.Exp, bias=mn[:, j:j + 1],
                                 accum_out=dn[:, j:j + 1])
                s.activation(es[:], es[:], ACT.Exp).then_inc(s_exp, 1)
            if u < 16:
                for e in range(2):
                    full(act_, ("t", u, e))
                    sb_ = slice(1, 2) if n == 0 else slice(0, 2)
                    view = ps[6 + e][:].rearrange("p (s i t) -> p s i t", s=2, i=2)
                    free(s.activation(PTs[e][:, sb_], view[:, sb_], ACT.Copy), ("t", u, e))
                full(act_, ("pv", u))
                s.activation(o_hi[:, 4 * p_ + 2 * gh:4 * p_ + 2 * gh + 2, n * P:(n + 1) * P],
                             ps[u % 4][:, 0:256].rearrange("p (i t) -> p i t", i=2), ACT.Copy).then_inc(ob_hi, 1)
        gates(N_GB, "gb", 1)
        for k in range(KD):
            full(act_, ("M", k))
            s.activation(mT_hi[:, k, :], ps[bank_of[("M", k)]][:, 0:MEM], ACT.Copy).then_inc(m_hi, 1)
        used(act_, N_GB + 7)
        for k in range(KD):
            act_.wait_ge(merged_b, k + 1)
            s.activation(o_hi[:, k, :], merged[:, k, :], ACT.Copy).then_inc(mg_hi, 1)
        for c in range(2):
            split_to(N_MX + 2 * c + 3)
        for j in range(4):
            split_to(N_XK + j + 2)
            used(act_, N_XK + j)
            for i in range(2):
                free(s.activation(kx[:, 2 * j + i, :], ps[bank_of[("xk", 2 * j + i)]][:, 0:MEM], ACT.Copy), ("xk", 2 * j + i))
        for c in range(2):
            split_to(N_XV + 2 * c + 3)
            used(act_, N_XV + 2 * c + 1)
            for m in range(NM):
                free(s.activation(vx[:, m, 512 * c:512 * c + 512], ps[2 * c + m][:], ACT.Copy), ("xv", c, m))
        norm(1, res, lambda t: was_freed(act_, ("mx", 1, t)))
        to_hT(1)

        def q_evac(h):
            split_to(N_XQ + h + 2)
            used(act_, N_XQ + h)
            for i in range(2):
                free(s.activation(qx[h % 2][:, i, :], ps[bank_of[("xq", 2 * h + i)]][:], ACT.Copy), ("xq", 2 * h + i))
        q_evac(0)
        for h in range(XA_HEADS):
            for j in range(2):
                act_.wait_ge(xs_max, 2 * h + j + 1)
                for i in range(2):
                    ins = s.activation(Px[j][:, i, :], ps[4 + j][:, MEM * i:MEM * i + MEM], ACT.Exp,
                                       scale=XA_HD ** -0.5, bias=mn[:, 2 * j + i:2 * j + i + 1],
                                       accum_out=dn[:, 2 * j + i:2 * j + i + 1])
                free(ins, ("xs", h, j))
            if h + 1 < XA_HEADS:
                q_evac(h + 1)
            for j in range(2):
                full(act_, ("xt", h, j))
                view = ps[6 + j][:].rearrange("p (m i t) -> p m i t", m=2, i=2)
                free(s.activation(PTx[:, :, 2 * j:2 * j + 2, :], view, ACT.Copy), ("xt", h, j))
            for c in range(2):
                full(act_, ("xo", h, c))
                s.activation(o_hi[:, 2 * h + c, :], ps[2 * (h % 2) + c][:], ACT.Copy).then_inc(xo_hi, 1)
        split_to(N_DENSE)
        for h in (2, 3):
            for c in range(2):
                was_freed(act_, ("xo", h, c))
        for q in range(3):
            act_.dma_start(biasf[32 * q:32 * q + 32, 0:2 * FF], b_gate_up[0]).then_inc(bf_in, 16)
            act_.dma_start(biasf[32 * q:32 * q + 32, 2 * FF:3 * FF], b_down[0]).then_inc(bf_in, 16)
        act_.dma_start(gbc[:], bass.AP(norm_ffn.tensor, 0, [[0, P], [1, D]])).then_inc(rt_in, 16)
        act_.dma_start(wr[:], w_router[0].rearrange("(k p) e -> p k e", p=P)).then_inc(rt_in, 16)
        act_.dma_start(br[:], bass.AP(b_router.tensor, 0, [[0, P], [1, E]])).then_inc(rt_in, 16)
        norm(2, res, lambda t: was_freed(act_, ("wo", 1, t)))
        act_.wait_ge(rt_in, 48)
        s.activation(wr_hi[:], wr[:], ACT.Copy).then_inc(wr_hi_s, 1)
        to_hT(2)
        act_.wait_ge(ex_in, 1)
        s.activation(ex[:], ex[:], ACT.Exp).then_inc(ex_out, 1)

        act_.wait_ge(list_ready, 1)
        nb = act_.value_load(nb_i[0:1, 0:1], min_val=MINB, max_val=MAXB - 1)
        used(act_, N_DENSE - 1)

        act_.wait_ge(biasS_ready, 1)

        def xg_hi(cnt):
            for q in range(2):
                act_.wait_ge(xgT_full, cnt + q + 1)
                s.activation(xgT_hi[:, 4 * q:4 * q + 4, :], ps[q][:].rearrange("p (k t) -> p k t", k=4),
                             ACT.Copy).then_inc(xgT_hi_r, 1)

        def y_copies(k):
            act_.wait_ge(idy_ready, k + 1)
            for oc in range(2):
                act_.wait_ge(m_used, k * WPB + M_HI - 1 + oc)
                s.activation(ysb[:, 512 * oc:512 * oc + 512], ps[4 + oc][:], ACT.Copy).then_inc(y_copied, 1)
        xg_hi(0)
        with act_.Fori(0, nb) as k:
            def hi(*js):
                for j in js:
                    act_.wait_ge(m_raw[j % M_RAW], k * (16 * WPB // M_RAW) + 16 * (j // M_RAW + 1))
                    act_.wait_ge(m_used, k * WPB + j + 1)
                    s.activation(m_hi_at[j % M_HI][:], m_raw_at[j % M_RAW][:], ACT.Copy).then_inc(m_hid, 1)

            def gate(half):
                act_.wait_ge(gmin, k * 2 + half + 1)
                s.activation(sig[:, 512 * half:512 * half + 512], glu[:, 512 * half:512 * half + 512],
                             ACT.Sigmoid, scale=ALPHA).then_inc(gsig, 1)

            def aT(half):
                act_.wait_ge(aT_full, k * 2 + half + 1)
                s.activation(aT_hi[:, 4 * half:4 * half + 4, :], ps[6 + half][:].rearrange("p (k t) -> p k t", k=4),
                             ACT.Copy).then_inc(aT_hi_r, 1)
            hi(0, 1)
            y_copies(k)
            hi(2, 3, 4, 5)
            gate(0)
            hi(6, 7, 8)
            aT(0)
            hi(9)
            gate(1)
            hi(10, 11)
            aT(1)
            xg_hi(k * 2 + 2)
        y_copies(nb)
        act_.wait_ge(y_out, nb * 16 + 16)
        act_.wait_ge(xg_in, nb * 16 + 16)
        act_.wait_ge(xgT_ready, nb * 2 + 2)
        act_.sem_inc(blocks_done, 1)
        act_.wait_ge(h3_out, 16 * NT)
        act_.dma_start(gfin[:], bass.AP(norm_final.tensor, 0, [[0, P], [1, D]])).then_inc(fin_in, 16)
        for t in range(NT):
            act_.wait_ge(yg_used, TOPK * (t + 1))
            s.activation(fin[:, t, :], res[:, t, :], ACT.Square, accum_out=ss[:, t:t + 1]).then_inc(fin_sq, 1)

    @block.vector
    def _(dve):
        v = nc.vector
        ck = Chain()

        def step(ins):
            ck.inc(ins, dve_step)
            ck.last(dve, dve_step)

        nxt = [0]

        def split_to(n):
            while nxt[0] <= min(n, N_DENSE - 1):
                m = nxt[0]
                nxt[0] += 1
                dve.wait_ge(hi_done[m % RING], m // RING + 1)
                v.tensor_tensor(wlo[m % RING][:], raw[m % RING][:], whi[m % RING][:].bitcast(F32),
                                ALU.subtract).then_inc(lo_done[m % RING], 1)

        def norm(stage, src):
            for t in range(NT):
                dve.wait_ge(rstd, NT * stage + t + 1)
                v.tensor_scalar(xn[:, t, :], src[:, t, :], rs[:, t:t + 1], None, ALU.mult).then_inc(xn_ready, 1)

        def to_hT(stage):
            for k in range(KD):
                key = ("T", stage, k)
                dve.wait_ge(hT_hi_ready, KD * stage + k + 1)
                ins = v.scalar_tensor_tensor(out=hT_lo[:, k, :], in0=ps[bank_of[key]][:], scalar=gain[stage][:, k:k + 1],
                                             in1=hT_hi[:, k, :].bitcast(F32), op0=ALU.mult, op1=ALU.subtract)
                free(ins, key)

        norm(0, x0)
        dve.wait_ge(gain_in, 16)
        to_hT(0)
        split_to(1)
        dve.wait_ge(const_in, 144)
        step(v.tensor_tensor(lbt[:], lbl[:, 0, :], lbl[:, 1, :], ALU.max))
        step(v.tensor_tensor(lbl[:, 0, :], lbl[:, 0, :], lbt[:], ALU.subtract))
        step(v.tensor_tensor(lbl[:, 1, :], lbl[:, 1, :], lbt[:], ALU.subtract))
        dve.wait_ge(pool_const, 2)
        for b in range(T5_BUCKETS):
            ds_ = [d for d in range(WINDOW) if t5_bucket_of(d) == b]
            if ds_:
                j0, n = 255 - ds_[-1], len(ds_)
                ins = v.tensor_copy(line[0:SWA_HEADS, j0:j0 + n], t5T[0:SWA_HEADS, b:b + 1].to_broadcast([SWA_HEADS, n]))
        ins.then_inc(line_in, 1)
        dve.wait_ge(act_step, 1)
        step(v.tensor_tensor(lbt[:], lbl[:, 0, :], lbl[:, 1, :], ALU.add))
        step(v.reciprocal(lbt[:], lbt[:]))
        step(v.tensor_tensor(lb[:], lbl[:, 0, :], lbt[:], ALU.mult))
        step(v.tensor_tensor(oml[:], lbl[:, 1, :], lbt[:], ALU.mult))
        for c in range(2):
            split_to(N_V + 2 * c + 3)

        def hgrn(hp):
            for h in (2 * hp, 2 * hp + 1):
                b = h % 4
                full(dve, ("L", h, 0))
                if h:
                    full(dve, ("O", h - 1))
                ins = v.tensor_tensor(A[:].rearrange("p (c t) -> p c t", c=4), ps[4][:].rearrange("p (c t) -> p c t", c=4),
                                      ident_bc, ALU.mult)
                free(ins, ("L", h, 0))
                yield
                for i, c in enumerate(LEVELS):
                    n = 7 * h + i
                    L = lev[n % 2]
                    Lv = L[:].rearrange("p (b c) -> p b c", c=2 * c)
                    Kv = hk[b][:].rearrange("p (b c) -> p b c", c=2 * c)
                    Qv = hq[b][:].rearrange("p (b c) -> p b c", c=2 * c)
                    dve.wait_ge(lev_exp, n + 1)
                    v.tensor_tensor(Lv[:, :, 0:c], Lv[:, :, 0:c], Kv[:, :, 0:c], ALU.mult)
                    v.tensor_tensor(Lv[:, :, c:2 * c], Lv[:, :, c:2 * c], Qv[:, :, c:2 * c], ALU.mult).then_inc(lev_ready, 1)
                    if i == 0:
                        dve.wait_ge(eg_ready, h + 1)
                        v.tensor_copy(dec[:], EG[:].rearrange("p (c t) -> p c t", t=P)[:, :, P - 1]).then_inc(dec_ready, 1)
                    if i > 0:
                        take(h, i - 1)
                    yield
                    if i == 0:
                        yield
                        if h % 2:
                            yield from x_part(h - 1)
                    if i == 2:
                        full(dve, ("S", h))
                        dve.wait_ge(dec_ready, h + 1)
                        sv_ = ps[7][:, 0:3 * P]
                        v.tensor_copy(ST[:, 0:P], sv_[:, 0:P]).then_inc(m_chain, 1)
                        dve.wait_ge(m_chain, 2 * h + 1)
                        v.scalar_tensor_tensor(out=ST[:, P:2 * P], in0=ST[:, 0:P], scalar=dec[:, 1:2], in1=sv_[:, P:2 * P],
                                               op0=ALU.mult, op1=ALU.add).then_inc(m_chain, 1)
                        dve.wait_ge(m_chain, 2 * h + 2)
                        ins = v.scalar_tensor_tensor(out=ST[:, 2 * P:3 * P], in0=ST[:, P:2 * P], scalar=dec[:, 2:3],
                                                     in1=sv_[:, 2 * P:3 * P], op0=ALU.mult, op1=ALU.add)
                        free(ins, ("S", h))
                        yield
                take(h, 6)
                dve.wait_ge(o_sq, h + 1)
                v.tensor_reduce(ss[:, 0:NT], ON[:].rearrange("p (c t) -> p c t", t=P), AX, ALU.add).then_inc(o_ss, 1)
                dve.wait_ge(o_rs, h + 1)
                ins = v.tensor_tensor(ON[:].rearrange("p (c t) -> p c t", t=P), ps[6][:].rearrange("p (c t) -> p c t", t=P),
                                      rs[:, 0:NT].rearrange("p (c a) -> p c a", a=1).to_broadcast([P, NT, P]), ALU.mult)
                free(ins, ("O", h))
                yield
            yield from x_part(2 * hp + 1)

        def take(h, i):
            c = LEVELS[i]
            key = ("L", h, i + 1)
            full(dve, key)
            was_freed(dve, ("L", h, i))
            src = ps[bank_of[key]][:].rearrange("p (b c) -> p b c", c=2 * c)[:, :, c:2 * c]
            dst = A[:].rearrange("p (b c) -> p b c", c=2 * c)[:, :, c:2 * c]
            ins = v.copy_predicated(dst, lmask[:, i, :].rearrange("p (b c) -> p b c", c=c), src)
            free(ins, key)

        def x_part(h):
            full(dve, ("X", h))
            free(v.scalar_tensor_tensor(out=ON[:], in0=ps[7][:], scalar=hgain[:, 0:1], in1=hs[h % 4][:],
                                        op0=ALU.mult, op1=ALU.mult), ("X", h))
            dve.wait_ge(o_hi_ready, h + 1)
            v.tensor_tensor(o_lo[:, h, :], ON[:], o_hi[:, h, :].bitcast(F32), ALU.subtract).then_inc(o_ready, 1)
            yield

        def advance(gen, n):
            for _ in range(n):
                next(gen, None)
        ident_bc = ident[:].rearrange("p (a t) -> p a t", a=1).to_broadcast([P, 4, P])
        filler = iter(())
        for hp in range(HG_PAIRS):
            n0 = N_HG + 3 * hp
            b0 = (2 * hp) % 4
            advance(filler, 8)
            split_to(n0 + 2)
            for i in range(2):
                h = 2 * hp + i
                dve.wait_ge(bank_free[bank_of[("f", h)]], ordinal[("f", h)] + 1)
                dve.wait_ge(act_step, 1 + h + 1)
                step(v.tensor_scalar(hG[b0 + i][:], hG[b0 + i][:], oml[:, h:h + 1], lb[:, h:h + 1], ALU.mult, ALU.add))
                v.tensor_scalar(hk[b0 + i][:], hk[b0 + i][:], oml[:, h:h + 1], None, ALU.mult).then_inc(f_sig, 1)
                v.tensor_scalar(hG[b0 + i][:], hG[b0 + i][:], 2.0 ** -63, None, ALU.max).then_inc(f_gate, 1)
            advance(filler, 8)
            split_to(n0 + 3)
            for i in range(2):
                h = 2 * hp + i
                dve.wait_ge(q_sig, h + 1)
                ins = v.tensor_tensor(hq[b0 + i][:], ps[bank_of[("q", h)]][:], hq[b0 + i][:], ALU.mult)
                free(ins, ("q", h))
            advance(filler, 8)
            split_to(n0 + 4)
            for i in range(2):
                h = 2 * hp + i
                dve.wait_ge(g_sig, h + 1)
                ins = v.tensor_tensor(hs[b0 + i][:], ps[bank_of[("g", h)]][:], hs[b0 + i][:], ALU.mult)
                free(ins, ("g", h))
            for i in range(2):
                h = 2 * hp + i
                dve.wait_ge(log_f, h + 1)
                v.tensor_tensor_scan(hG[b0 + i][:], scan1[:], hG[b0 + i][:], 0.0, ALU.mult, ALU.add).then_inc(G_ready, 1)
            advance(filler, 99)
            filler = hgrn(hp)
        for j in range(4):
            advance(filler, 6)
            split_to(N_SQ + j + 2)
        advance(filler, 99)
        split_to(N_GA + 2)

        for m in range(4):
            split_to(N_GA + 2 * m + 3)
            used(dve, N_GA + 2 * m + 1)
            for i in range(2):
                k = 2 * m + i
                dve.wait_ge(bank_free[bank_of[("ga", k)]], ordinal[("ga", k)] + 1)
                free(v.tensor_tensor(merged[:, k, :], ps[bank_of[("wa", k)]][:], GATE[k % 2][:], ALU.mult), ("wa", k))

        split_to(N_GB + 2)
        dve.wait_ge(bias_in, 32)
        for u in range(17):
            if u < 16:
                p_, gh, n = u // 8, (u // 4) % 2, u % 4
                w0 = P if n == 0 else 0
                for e in range(2):
                    full(dve, ("s", u, e))
                    if u:
                        full(dve, ("t", u - 1, e))
                    src = ps[4 + e][:].rearrange("p (i s) -> p i s", i=2)[:, :, w0:256]
                    ins = v.scalar_tensor_tensor(out=Ss[:, 2 * e:2 * e + 2, w0:256], in0=src, scalar=SWA_HD ** -0.5,
                                                 in1=bias[p_][:, 4 * e + 2 * gh:4 * e + 2 * gh + 2, w0:256],
                                                 op0=ALU.mult, op1=ALU.add)
                    free(ins, ("s", u, e))
                for e in range(2):
                    dve.wait_ge(bank_free[4 + e], ordinal[("s", u, e)] + 1)
                step(v.tensor_reduce(mx[:], Ss[:, :, w0:256], AX, ALU.max))
                snk = sinks[:, 8 * p_:8 * p_ + 8].rearrange("p (e g) -> p e g", e=2)[:, :, 2 * gh:2 * gh + 2]
                m2 = mx[:].rearrange("p (e g) -> p e g", e=2)
                step(v.tensor_tensor(m2, m2, snk, ALU.max))
                step(v.tensor_tensor(es[:].rearrange("p (e g) -> p e g", e=2), snk, m2, ALU.subtract))
                v.tensor_scalar(mn[:], mx[:], -1.0, None, ALU.mult).then_inc(s_max, 1)
                dve.wait_ge(s_exp, u + 1)
                step(v.tensor_tensor(dn[:], dn[:], es[:], ALU.add))
                step(v.reciprocal(rd[:], dn[:]))
                v.tensor_tensor(Ss[:, :, w0:256], Ss[:, :, w0:256],
                                rd[:].rearrange("p (j a) -> p j a", a=1).to_broadcast([P, 4, 256 - w0]),
                                ALU.mult).then_inc(s_norm, 1)
            if u >= 1:
                w = u - 1
                p_, gh, n = w // 8, (w // 4) % 2, w % 4
                dve.wait_ge(ob_hi, w + 1)
                ins = v.tensor_tensor(o_lo[:, 4 * p_ + 2 * gh:4 * p_ + 2 * gh + 2, n * P:(n + 1) * P],
                                      ps[w % 4][:, 0:256].rearrange("p (i t) -> p i t", i=2),
                                      o_hi[:, 4 * p_ + 2 * gh:4 * p_ + 2 * gh + 2, n * P:(n + 1) * P].bitcast(F32),
                                      ALU.subtract)
                free(ins, ("pv", w))

        for m in range(4):
            split_to(N_GB + 2 * m + 3)
            used(dve, N_GB + 2 * m + 1)
            for i in range(2):
                k = 2 * m + i
                dve.wait_ge(bank_free[bank_of[("gb", k)]], ordinal[("gb", k)] + 1)
                g_ = GATE[k % 2]
                ins = v.tensor_tensor(g_[:], ps[bank_of[("wb", k)]][:], g_[:], ALU.mult)
                free(ins, ("wb", k))
                dve.wait_ge(bank_free[bank_of[("wb", k)]], ordinal[("wb", k)] + 1)
                v.tensor_tensor(merged[:, k, :], merged[:, k, :], g_[:], ALU.add).then_inc(merged_b, 1)
        for k in range(KD):
            key = ("M", k)
            dve.wait_ge(m_hi, k + 1)
            free(v.tensor_tensor(mT_lo[:, k, :], ps[bank_of[key]][:, 0:MEM], mT_hi[:, k, :].bitcast(F32), ALU.subtract), key)
        for k in range(KD):
            dve.wait_ge(mg_hi, k + 1)
            v.tensor_tensor(o_lo[:, k, :], merged[:, k, :], o_hi[:, k, :].bitcast(F32), ALU.subtract).then_inc(mg_ready, 1)
        for c in range(2):
            split_to(N_MX + 2 * c + 3)
            used(dve, N_MX + 2 * c + 1)
            dve.wait_ge(res_in, 16)
            for t in range(NT):
                r = res[:, t, 512 * c:512 * c + 512]
                free(v.tensor_tensor(r, ps[t][:], r, ALU.add), ("mx", c, t))
        for j in range(4):
            split_to(N_XK + j + 2)
        for c in range(2):
            split_to(N_XV + 2 * c + 3)
        norm(1, res)
        to_hT(1)

        def lo_out(h):
            for c in range(2):
                dve.wait_ge(xo_hi, 2 * h + c + 1)
                bk = 2 * (h % 2) + c
                free(v.tensor_tensor(o_lo[:, 2 * h + c, :], ps[bk][:], o_hi[:, 2 * h + c, :].bitcast(F32),
                                     ALU.subtract), ("xo", h, c))
        split_to(N_XQ + 2)
        for h in range(XA_HEADS):
            for j in range(2):
                full(dve, ("xs", h, j))
                step(v.tensor_reduce(mx[:, 2 * j:2 * j + 2], ps[4 + j][:].rearrange("p (i s) -> p i s", i=2), AX, ALU.max))
                v.tensor_scalar(mn[:, 2 * j:2 * j + 2], mx[:, 2 * j:2 * j + 2], -(XA_HD ** -0.5), None,
                                ALU.mult).then_inc(xs_max, 1)
            for j in range(2):
                was_freed(dve, ("xs", h, j))
                step(v.reciprocal(rd[:, 2 * j:2 * j + 2], dn[:, 2 * j:2 * j + 2]))
                v.tensor_tensor(Px[j][:], Px[j][:], rd[:, 2 * j:2 * j + 2].rearrange("p (i a) -> p i a", a=1)
                                .to_broadcast([P, 2, MEM]), ALU.mult).then_inc(xs_norm, 1)
            split_to(N_XQ + h + 3)
            lo_out(h)
        split_to(N_DENSE)
        for c in range(2):
            used(dve, N_WO + 2 * c + 1)
            for t in range(NT):
                r = res[:, t, 512 * c:512 * c + 512]
                free(v.tensor_tensor(r, ps[t][:], r, ALU.add), ("wo", c, t))
        norm(2, res)
        dve.wait_ge(wr_hi_s, 1)
        v.tensor_tensor(wr_lo[:], wr[:], wr_hi[:].bitcast(F32), ALU.subtract).then_inc(wr_ready, 1)
        to_hT(2)
        for t in range(NT):
            dve.wait_ge(xn_ready, 2 * NT + t + 1)
            v.tensor_tensor(h3g[:, t, :], xn[:, t, :], gbc[:], ALU.mult).then_inc(h3g_ready, 1)

        full(dve, ("rt", 0))
        free(v.tensor_copy(lgT[0:E, :], ps[0][0:E, :]), ("rt", 0))
        full(dve, ("rl", 0))
        lg3 = ps[3][:, 0:NT * E].rearrange("p (t e) -> p t e", t=NT)
        ins = v.tensor_tensor(lg[:], lg3, br[:].rearrange("p (a e) -> p a e", a=1).to_broadcast([P, NT, E]), ALU.add)
        step(ins)
        dve.sem_inc(bank_free[3], 1)
        for t in range(NT):
            ins = v.max(v8[:, t, :], lg[:, t, :])
        step(ins)

        def bc(ap2):
            return ap2.rearrange("p (t a) -> p t a", a=1).to_broadcast([P, NT, E])
        v4 = v8[:, :, TOPK - 1:TOPK].to_broadcast([P, NT, E])
        v1 = v8[:, :, 0:1].to_broadcast([P, NT, E])
        v.tensor_tensor(ex[:], lg[:], v1, ALU.subtract).then_inc(ex_in, 1)
        v.tensor_tensor(gt[:], lg[:], v4, ALU.is_gt)
        step(v.tensor_tensor(eq[:], lg[:], v4, ALU.is_equal))
        step(v.tensor_reduce(need[:], gt[:], AX, ALU.add))
        for t in range(NT):
            ins = v.tensor_tensor_scan(cs[:, t, :], scan1[:, 1:1 + E], eq[:, t, :], 0.0, ALU.mult, ALU.add)
        step(ins)
        step(v.tensor_tensor(cs[:], cs[:], bc(need[:]), ALU.add))
        step(v.scalar_tensor_tensor(out=ch[:], in0=cs[:], scalar=float(TOPK), in1=eq[:], op0=ALU.is_le, op1=ALU.mult))
        step(v.tensor_tensor(ch[:], ch[:], gt[:], ALU.add))
        v.tensor_copy(chb[:], ch[:]).then_inc(ch_ready, 1)
        dve.wait_ge(ex_out, 1)
        step(v.tensor_tensor(ex[:], ex[:], ch[:], ALU.mult))
        step(v.tensor_reduce(den[:], ex[:], AX, ALU.add))
        step(v.reciprocal(den[:], den[:]))
        step(v.tensor_tensor(ex[:], ex[:], bc(den[:]), ALU.mult))
        for t in range(NT):
            ins = v.tensor_tensor_scan(cs[:, t, :], scan1[:, 1:1 + E], ch[:, t, :], 0.0, ALU.mult, ALU.add)
        step(ins)
        full(dve, ("cn", 0))
        step(v.tensor_copy(cnt[:], ps[2][:, 0:E]))
        step(v.tensor_scalar(nbe[:], cnt[:], 0.0, None, ALU.is_gt))
        for i in range(1, NT):
            step(v.scalar_tensor_tensor(out=nbe[:], in0=cnt[:], scalar=float(P * i), in1=nbe[:], op0=ALU.is_gt, op1=ALU.add))
        step(v.tensor_scalar(nbe[:, 0:1], nbe[:, 0:1], 1.0, None, ALU.max))
        step(v.tensor_tensor_scan(bend[:], scan1[:, 1:1 + E], nbe[:], 0.0, ALU.mult, ALU.add))
        step(v.tensor_tensor(bst[:], bend[:], nbe[:], ALU.subtract))
        full(dve, ("ps", 0))
        step(v.tensor_copy(pos[:], ps[1][:, 0:NT * E].rearrange("p (t e) -> p t e", t=NT)))
        step(v.tensor_scalar(bq[:], pos[:], float(P), None, ALU.is_ge))
        for i in range(2, NT):
            step(v.scalar_tensor_tensor(out=bq[:], in0=pos[:], scalar=float(P * i), in1=bq[:], op0=ALU.is_ge, op1=ALU.add))
        step(v.scalar_tensor_tensor(out=pos[:], in0=bq[:], scalar=-float(P), in1=pos[:], op0=ALU.mult, op1=ALU.add))
        step(v.tensor_tensor(bq[:], bq[:], bst[:].rearrange("p (a e) -> p a e", a=1).to_broadcast([P, NT, E]), ALU.add))
        for r in range(TOPK):
            step(v.scalar_tensor_tensor(out=oh[:], in0=cs[:], scalar=float(r + 1), in1=ch[:], op0=ALU.is_equal, op1=ALU.mult))
            for src, dst in ((bq, BL), (pos, JJ), (ex, GT)):
                step(v.tensor_tensor(tmp4[:], oh[:], src[:], ALU.mult))
                step(v.tensor_reduce(dst[:, :, r], tmp4[:], AX, ALU.add))
        dve.wait_ge(disp_const, 1)
        for i in range(NT * TOPK):
            t, r = divmod(i, TOPK)
            if i >= 2:
                dve.wait_ge(list_mm, i - 1)
            v.tensor_scalar(ohj[i % 2][:], ioj[:], JJ[:, t, r:r + 1], None, ALU.is_equal)
            v.tensor_scalar(ohb[i % 2][:, 0, :], iob[:], BL[:, t, r:r + 1], tokid[:, t:t + 1], ALU.is_equal, ALU.mult)
            v.tensor_scalar(ohb[i % 2][:, 1, :], iob[:], BL[:, t, r:r + 1], tokid4[:, t, r:r + 1], ALU.is_equal,
                            ALU.mult).then_inc(onehot, 1)
        bg = big[:]
        step(v.tensor_tensor(bg, iob[:].rearrange("p (b a) -> p b a", a=1).to_broadcast([P, MAXB, E]),
                             bend[:].rearrange("p (a e) -> p a e", a=1).to_broadcast([P, MAXB, E]), ALU.is_ge))
        step(v.tensor_reduce(bex[:], bg, AX, ALU.add))
        step(v.tensor_scalar(bex[:], bex[:], float(E - 1), None, ALU.min))
        step(v.tensor_copy(bex_i[:], bex[:]))
        step(v.tensor_copy(nb_i[:], bend[:, E - 1:E]))
        step(v.tensor_scalar(selb[0:96, :], bex[0:96, :], pm[0:96, 0:1], None, ALU.is_equal))
        dve.wait_ge(list_mm, NT * TOPK)
        step(v.tensor_scalar(lists[:], ps[3][:, 0:2 * MAXB].rearrange("p (a b) -> p a b", a=2), -1.0, None, ALU.add))
        step(v.tensor_scalar(empty[:], lists[:], 0.0, float(SKIP), ALU.is_lt, ALU.mult))
        step(v.tensor_tensor(lists[:], lists[:], empty[:], ALU.add))
        step(v.tensor_copy(lists_i[:], lists[:]))
        dve.sem_inc(list_ready, 1)

        dve.wait_ge(list_ready, 1)
        v.memset(xg[:], 0.0).then_inc(xg_clear, 1)
        v.tensor_copy(idx[:], lists_i[:, 0, 0:1]).then_inc(idx_ready, 1)
        nb = dve.value_load(nb_i[0:1, 0:1], min_val=MINB, max_val=MAXB - 1)
        v.memset(idy[:], SKIP).then_inc(idy_ready, 1)
        dve.sem_inc(m_lod_v, WPB - len(POOL_LO))

        def xg_lo(cnt_hi):
            for q in range(2):
                dve.wait_ge(xgT_hi_r, cnt_hi + q + 1)
                v.tensor_tensor(xgT_lo[:, 4 * q:4 * q + 4, :], ps[q][:].rearrange("p (k t) -> p k t", k=4),
                                xgT_hi[:, 4 * q:4 * q + 4, :].bitcast(F32), ALU.subtract).then_inc(xgT_ready, 1)
        xg_lo(0)
        with dve.Fori(0, nb) as k:
            def lo(*js):
                for j in js:
                    make_low(dve, v, k, j)

            def glu_min(half):
                hs_ = slice(512 * half, 512 * half + 512)
                dve.wait_ge(m_used, k * WPB + 4 * half + 2 + M_HI)
                v.tensor_scalar(glu[:, hs_], ps[2 * half][:], LIMIT, None, ALU.min).then_inc(gmin, 1)

            def swiglu(half):
                hs_ = slice(512 * half, 512 * half + 512)
                dve.wait_ge(m_used, k * WPB + 4 * half + 4 + M_HI)
                v.tensor_scalar(act[:, hs_], ps[2 * half + 1][:], LIMIT, -LIMIT, ALU.min, ALU.max).then_inc(glu_free, 1)
                dve.wait_ge(gmin, k * 2 + half + 1)
                dve.wait_ge(glu_free, k * 4 + 2 * half + 1)
                v.scalar_tensor_tensor(out=act[:, hs_], in0=act[:, hs_], scalar=1.0, in1=glu[:, hs_],
                                       op0=ALU.add, op1=ALU.mult).then_inc(glu_free, 1)
                dve.wait_ge(glu_free, k * 4 + 2 * half + 2)
                dve.wait_ge(gsig, k * 2 + half + 1)
                v.tensor_tensor(act[:, hs_], act[:, hs_], sig[:, hs_], ALU.mult).then_inc(act_ready, 1)

            def aT(half):
                dve.wait_ge(aT_hi_r, k * 2 + half + 1)
                v.tensor_tensor(aT_lo[:, 4 * half:4 * half + 4, :], ps[6 + half][:].rearrange("p (k t) -> p k t", k=4),
                                aT_hi[:, 4 * half:4 * half + 4, :].bitcast(F32), ALU.subtract).then_inc(aT_ready, 1)
            lo(0)
            dve.wait_ge(m_used, k * WPB + M_HI - 2)
            v.tensor_copy(selt[0:96, :], selb[0:96, bass.ds(k, 1)].to_broadcast([96, P])).then_inc(sel_ready, 1)
            dve.wait_ge(xg_in, k * 16 + 16)
            v.tensor_copy(idx[:], lists_i[:, 0, bass.ds(k + 1, 1)]).then_inc(idx_ready, 1)
            lo(1, 2, 3)
            glu_min(0)
            lo(4)
            swiglu(0)
            lo(6, 7)
            aT(0)
            glu_min(1)
            dve.wait_ge(y_out, k * 16 + 16)
            v.tensor_copy(idy[:], lists_i[:, 1, bass.ds(k, 1)]).then_inc(idy_ready, 1)
            lo(8)
            swiglu(1)
            lo(10)
            aT(1)
            lo(11)
            xg_lo(k * 2 + 2)

        for i in range(NT * TOPK):
            t, r = divmod(i, TOPK)
            dve.wait_ge(yg_in[i % 8], 16 * (i // 8 + 1))
            v.scalar_tensor_tensor(out=res[:, t, :], in0=yg[i % 8][:], scalar=GT[:, t, r:r + 1], in1=res[:, t, :],
                                   op0=ALU.mult, op1=ALU.add).then_inc(yg_used, 1)
            dve.wait_ge(yg_used, i + 1)
        dve.wait_ge(fin_in, 16)
        for t in range(NT):
            dve.wait_ge(fin_rs, t + 1)
            v.scalar_tensor_tensor(out=fin[:, t, :], in0=res[:, t, :], scalar=rs[:, t:t + 1], in1=gfin[:],
                                   op0=ALU.mult, op1=ALU.mult).then_inc(fin_ready, 1)

    @block.tensor
    def _(pe):
        mm = nc.tensor.matmul

        def slot_ready(n):
            pe.wait_ge(lo_done[n % RING], n // RING + 1)

        def three(out_, l_hi, l_lo, r_hi, r_lo, first, last):
            mm(out_, l_hi, r_hi, start=first, stop=False)
            mm(out_, l_hi, r_lo, start=False, stop=False)
            return mm(out_, l_lo, r_hi, start=False, stop=last)

        def w_stat(n, names, r_hi, r_lo, N=T, extra=None):
            slot_ready(n)
            for i, key in enumerate(names):
                opened(pe, key)
                for k in range(KD):
                    def wv(w):
                        return w[:].rearrange("p (k c) -> p k c", c=256)[:, k, i * P:(i + 1) * P]
                    ins = three(ps[bank_of[key]][:, 0:N], wv(whi[n % RING]), wv(wlo[n % RING]),
                                r_hi[:, k, :], r_lo[:, k, :], k == 0, k == KD - 1)
                    if extra and k % 2 == 1 and not (i == 1 and k == KD - 1):
                        extra()
            ins.then_inc(w_used, 1)
            if extra:
                extra()

        def t_stat(n, kh, tiles, keys, l_hi, l_lo, before=None):
            slot_ready(n)
            for t in range(tiles):
                if kh == 0:
                    opened(pe, keys[t])
                for k in range(4):
                    wv = [w[:].rearrange("p (k c) -> p k c", c=512)[:, k, :] for w in (whi[n % RING], wlo[n % RING])]
                    kk = 4 * kh + k
                    if before:
                        before(kk)
                    ins = three(ps[bank_of[keys[t]]][:], h2(l_hi, kk, t), h2(l_lo, kk, t), wv[0], wv[1],
                                kh == 0 and k == 0, kh == 1 and k == 3)
            ins.then_inc(w_used, 1)

        def transposes(stage):
            for k in range(KD):
                key = ("T", stage, k)
                opened(pe, key)
                for t in range(NT):
                    if k == 0:
                        pe.wait_ge(xn_ready, NT * stage + t + 1)
                    ins = nc.tensor.transpose(ps[bank_of[key]][:, t * P:(t + 1) * P], xn[:, t, k * P:(k + 1) * P], ident[:])
                ins.then_inc(bank_full[bank_of[key]], 1)

        def done(ins, key):
            ins.then_inc(bank_full[bank_of[key]], 1)

        def after_free(key):
            was_freed(pe, key)

        pe.wait_ge(pool_const, 1)
        transposes(0)
        for k in range(4, KD):
            after_free(("T", 0, k))
        for c in range(2):
            for kh in range(2):
                t_stat(N_V + 2 * c + kh, kh, NT, [("v", c, t) for t in range(NT)], hT_hi, hT_lo)

        def hgrn(hp):
            for h in (2 * hp, 2 * hp + 1):
                b = h % 4
                q, k_ = hq[b], hk[b]
                key = ("L", h, 0)
                opened(pe, key)
                pe.wait_ge(f_sig, h + 1)
                after_free(("q", h))
                for c in range(NT):
                    ins = mm(ps[4][:, c * P:(c + 1) * P], k_[:, c * P:(c + 1) * P], q[:, c * P:(c + 1) * P], start=True, stop=True)
                done(ins, key)
                yield
                for i, half in enumerate(LEVELS):
                    n = 7 * h + i
                    key = ("L", h, i + 1)
                    opened(pe, key)
                    pe.wait_ge(lev_ready, n + 1)
                    L = lev[n % 2]
                    for c in range(NT):
                        cs_ = slice(c * P, (c + 1) * P)
                        rhs = L[:, cs_].rearrange("p (b c) -> p b c", c=2 * half)[:, :, half:]
                        o_ = ps[bank_of[key]][:, cs_].rearrange("p (b c) -> p b c", c=2 * half)[:, :, half:]
                        ins = mm(o_, L[:, cs_], rhs, start=True, stop=True)
                    done(ins, key)
                    yield
                    if i == 0:
                        key = ("K", h)
                        opened(pe, key)
                        pe.wait_ge(kd_ready, h + 1)
                        for c in range(3):
                            ins = nc.tensor.transpose(ps[6][:, c * P:(c + 1) * P], KDt[:, c * P:(c + 1) * P], ident[:])
                        done(ins, key)
                        yield
                        if h % 2:
                            yield from x_part(h - 1)
                    if i == 2:
                        key = ("S", h)
                        opened(pe, key)
                        after_free(("K", h))
                        for c in range(3):
                            ins = mm(ps[7][:, c * P:(c + 1) * P], KDT[:, c * P:(c + 1) * P], v_sb[:, c, h * P:(h + 1) * P],
                                     start=True, stop=True)
                        done(ins, key)
                        yield
                key = ("O", h)
                opened(pe, key)
                after_free(("L", h, 7))
                after_free(("S", h))
                pe.wait_ge(qe_ready, h + 1)
                for c in range(NT):
                    cs_ = slice(c * P, (c + 1) * P)
                    ins = mm(ps[6][:, cs_], A[:, cs_], v_sb[:, c, h * P:(h + 1) * P], start=True, stop=(c == 0))
                    if c:
                        ins = mm(ps[6][:, cs_], EG[:, cs_], ST[:, (c - 1) * P:c * P], start=False, stop=True)
                done(ins, key)
                yield
            yield from x_part(2 * hp + 1)

        def x_part(h):
            key = ("X", h)
            opened(pe, key)
            after_free(("O", h))
            for c in range(NT):
                ins = nc.tensor.transpose(ps[7][:, c * P:(c + 1) * P], ON[:, c * P:(c + 1) * P], ident[:])
            done(ins, key)
            yield

        filler = iter(())
        for hp in range(HG_PAIRS):
            n0 = N_HG + 3 * hp

            def extra():
                next(filler, None)
            for s_, name in enumerate("fqg"):
                w_stat(n0 + s_, [(name, 2 * hp), (name, 2 * hp + 1)], hT_hi, hT_lo, extra=extra)
            for _ in filler:
                pass
            filler = hgrn(hp)
        turn = [0]

        def extra3():
            turn[0] += 1
            if turn[0] % 4:
                next(filler, None)
        for j in range(4):
            w_stat(N_SQ + j, [("sq", 2 * j), ("sq", 2 * j + 1)], hT_hi, hT_lo, extra=extra3)
        for _ in filler:
            pass
        for m in range(4):
            w_stat(N_GA + 2 * m, [("ga", 2 * m), ("ga", 2 * m + 1)], hT_hi, hT_lo)
            if m == 0:
                pe.wait_ge(o_ready, HG_HEADS)
            w_stat(N_GA + 2 * m + 1, [("wa", 2 * m), ("wa", 2 * m + 1)], o_hi, o_lo)
        w_stat(N_SK, [("sk", 0), ("sk", 1)], hT_hi, hT_lo)
        slot_ready(N_SV)
        for i in range(2):
            key = ("sv", i)
            opened(pe, key)
            for t in (2 * i, 2 * i + 1):
                for k in range(KD):
                    wv = [w[:].rearrange("p (k c) -> p k c", c=256)[:, k, :] for w in (whi[N_SV % RING], wlo[N_SV % RING])]
                    ins = three(ps[bank_of[key]][:, 256 * (t % 2):256 * (t % 2) + 256], h2(hT_hi, k, t), h2(hT_lo, k, t),
                                wv[0], wv[1], k == 0, k == KD - 1)
        ins.then_inc(w_used, 1)

        for i in range(2):
            after_free(("sk", i))
            after_free(("sv", i))
        for u in range(17):
            if u < 16:
                p_, gh, n = u // 8, (u // 4) % 2, u % 4
                w0 = P if n == 0 else 0
                if n == 0:
                    for i in range(2):
                        after_free(("sq", 2 * (2 * p_ + gh) + i))
                for e in range(2):
                    key = ("s", u, e)
                    opened(pe, key)
                    rows = slice(64 * e, 64 * e + 64)
                    for i in range(2):
                        ins = mm(ps[4 + e][:, 256 * i + w0:256 * i + 256],
                                 qS[rows, 4 * p_ + 2 * gh + i, n * P:(n + 1) * P],
                                 kS[rows, p_, (n - 1) * P + w0:(n + 1) * P], start=True, stop=True)
                    done(ins, key)
            if u >= 1:
                w = u - 1
                p_, gh, n = w // 8, (w // 4) % 2, w % 4
                pe.wait_ge(s_norm, w + 1)
                sbs = (1,) if n == 0 else (0, 1)
                for e in range(2):
                    key = ("t", w, e)
                    opened(pe, key)
                    for s_ in sbs:
                        for i in range(2):
                            o0 = 256 * s_ + P * i
                            ins = nc.tensor.transpose(ps[6 + e][:, o0:o0 + P], Ss[:, 2 * e + i, P * s_:P * s_ + P], ident[:])
                    done(ins, key)
                key = ("pv", w)
                opened(pe, key)
                for e in range(2):
                    after_free(("t", w, e))
                    kv = 2 * p_ + e
                    for s_ in sbs:
                        ins = mm(ps[w % 4][64 * e:64 * e + 64, 0:256], vS[:, n - 1 + s_, kv * 64:kv * 64 + 64],
                                 PTs[e][:, s_].rearrange("p i t -> p (i t)"), start=(s_ == sbs[0]), stop=(s_ == 1))
                done(ins, key)
        for m in range(4):
            w_stat(N_GB + 2 * m, [("gb", 2 * m), ("gb", 2 * m + 1)], hT_hi, hT_lo)
            if m == 0:
                for w in range(12, 16):
                    after_free(("pv", w))
            w_stat(N_GB + 2 * m + 1, [("wb", 2 * m), ("wb", 2 * m + 1)], o_hi, o_lo)
        pe.wait_ge(mem_in, 16)
        for k in range(KD):
            key = ("M", k)
            opened(pe, key)
            for m in range(NM):
                ins = nc.tensor.transpose(ps[bank_of[key]][:, m * P:(m + 1) * P], memr[:, m, k * P:(k + 1) * P], ident[:])
            done(ins, key)
        pe.wait_ge(mg_ready, KD)
        for c in range(2):
            for kh in range(2):
                t_stat(N_MX + 2 * c + kh, kh, NT, [("mx", c, t) for t in range(NT)], o_hi, o_lo)
        for j in range(4):
            w_stat(N_XK + j, [("xk", 2 * j), ("xk", 2 * j + 1)], mT_hi, mT_lo, N=MEM)
        for c in range(2):
            for kh in range(2):
                t_stat(N_XV + 2 * c + kh, kh, NM, [("xv", c, m) for m in range(NM)], mT_hi, mT_lo)
        transposes(1)
        for k in range(4, KD):
            after_free(("T", 1, k))
        for c in range(2):
            for m in range(NM):
                after_free(("xv", c, m))
        for j in range(6, 8):
            after_free(("xk", j))

        def scores(h):
            for i in range(2):
                after_free(("xq", 2 * h + i))
            for j in range(2):
                key = ("xs", h, j)
                opened(pe, key)
                for i in range(2):
                    t = 2 * j + i
                    for c in range(2):
                        ins = mm(ps[4 + j][:, MEM * i:MEM * i + MEM], qx[h % 2][:, c, t * P:(t + 1) * P], kx[:, 2 * h + c, :],
                                 start=(c == 0), stop=(c == 1))
                done(ins, key)

        def mix(h):
            for j in range(2):
                key = ("xt", h, j)
                opened(pe, key)
                pe.wait_ge(xs_norm, 2 * h + j + 1)
                for m in range(NM):
                    for i in range(2):
                        o0 = 256 * m + P * i
                        ins = nc.tensor.transpose(ps[6 + j][:, o0:o0 + P], Px[j][:, i, m * P:(m + 1) * P], ident[:])
                done(ins, key)
            for j in range(2):
                after_free(("xt", h, j))
            for c in range(2):
                key = ("xo", h, c)
                opened(pe, key)
                for m in range(NM):
                    ins = mm(ps[2 * (h % 2) + c][:], vx[:, m, (2 * h + c) * P:(2 * h + c + 1) * P],
                             PTx[:, m].rearrange("p t c -> p (t c)"), start=(m == 0), stop=(m == NM - 1))
                done(ins, key)
        w_stat(N_XQ, [("xq", 0), ("xq", 1)], hT_hi, hT_lo)
        scores(0)
        for h in range(XA_HEADS):
            if h + 1 < XA_HEADS:
                w_stat(N_XQ + h + 1, [("xq", 2 * h + 2), ("xq", 2 * h + 3)], hT_hi, hT_lo)
            mix(h)
            if h + 1 < XA_HEADS:
                scores(h + 1)
        for h in (2, 3):
            for c in range(2):
                after_free(("xo", h, c))
        for c in range(2):
            for kh in range(2):
                t_stat(N_WO + 2 * c + kh, kh, NT, [("wo", c, t) for t in range(NT)], o_hi, o_lo)
        transposes(2)
        for k in range(4, KD):
            after_free(("T", 2, k))
        pe.wait_ge(wr_ready, 1)
        opened(pe, ("rt", 0))
        for k in range(KD):
            ins = three(ps[0][0:E, :], wr_hi[:, k, :], wr_lo[:, k, :], hT_hi[:, k, :], hT_lo[:, k, :], k == 0, k == KD - 1)
        done(ins, ("rt", 0))
        opened(pe, ("rl", 0))
        after_free(("rt", 0))
        for t in range(NT):
            ins = nc.tensor.transpose(ps[3][:, t * E:(t + 1) * E], lgT[0:E, t * P:(t + 1) * P], ident[0:E, 0:E])
        done(ins, ("rl", 0))
        pe.wait_ge(ch_ready, 1)
        pe.wait_ge(disp_const, 1)
        opened(pe, ("ps", 0))
        for t in range(NT):
            for t2 in range(t + 1):
                ins = mm(ps[1][:, t * E:(t + 1) * E], (U_lt if t2 == t else ones_b)[:], chb[:, t2, :],
                         start=(t2 == 0), stop=(t2 == t))
        done(ins, ("ps", 0))
        opened(pe, ("cn", 0))
        for t in range(NT):
            ins = mm(ps[2][:, 0:E], ones_b[:], chb[:, t, :], start=(t == 0), stop=(t == NT - 1))
        done(ins, ("cn", 0))
        opened(pe, ("tl", 0))
        for i in range(NT * TOPK):
            pe.wait_ge(onehot, i + 1)
            mm(ps[3][:, 0:2 * MAXB], ohj[i % 2][:], ohb[i % 2][:].rearrange("p a b -> p (a b)"), start=(i == 0), stop=(i == NT * TOPK - 1)).then_inc(list_mm, 1)

        pe.wait_ge(list_ready, 1)
        pe.wait_ge(biasS_ready, 1)
        nb = pe.value_load(nb_i[0:1, 0:1], min_val=MINB, max_val=MAXB - 1)
        for k in range(4, KD):
            after_free(("T", 2, k))

        def xg_transposes():
            for q in range(2):
                for i in range(4):
                    kk = 4 * q + i
                    ins = nc.tensor.transpose(ps[q][:, i * P:(i + 1) * P], xg[:, kk * P:(kk + 1) * P], ident[:])
                ins.then_inc(xgT_full, 1)
        pe.wait_ge(xg_in, 16)
        xg_transposes()
        pe.sem_inc(m_used, M_HI)
        pe.wait_ge(xgT_ready, 2)
        with pe.Fori(0, nb) as k:
            def act_transposes(half):
                pe.wait_ge(act_ready, k * 2 + half + 1)
                for i in range(4):
                    kk = 4 * half + i
                    ins = nc.tensor.transpose(ps[6 + half][:, i * P:(i + 1) * P], act[:, kk * P:(kk + 1) * P], ident[:])
                ins.then_inc(aT_full, 1)
            for j in range(WPB):
                if j < 8:
                    c, kh = divmod(j, 2)
                    bank, l_hi, l_lo, b0 = ps[c], xgT_hi, xgT_lo, (c % 2) * FF + (c // 2) * 512
                else:
                    kh, oc = divmod(j - 8, 2)
                    bank, l_hi, l_lo, b0 = ps[4 + oc], aT_hi, aT_lo, 2 * FF + oc * 512
                if j == 0:
                    pe.wait_ge(sel_ready, k + 1)
                if j == 8:
                    pe.wait_ge(y_copied, k * 2 + 2)
                    pe.wait_ge(aT_ready, k * 2 + 1)
                if j == 10:
                    pe.wait_ge(aT_ready, k * 2 + 2)
                if kh == 0:
                    mm(bank[:], selt[0:96, :], biasS[0:96, b0:b0 + 512], start=True, stop=False)
                m_low(pe, k, j)
                wv = [w[:].rearrange("p (k c) -> p k c", c=512) for w in (m_hi_at[j % M_HI], m_lo_at[j % M_LO])]
                for i in range(4):
                    ins = three(bank[:], l_hi[:, 4 * kh + i, :], l_lo[:, 4 * kh + i, :], wv[0][:, i, :], wv[1][:, i, :],
                                False, kh == 1 and i == 3)
                ins.then_inc(m_used, 1)
                if j == 5:
                    act_transposes(0)
                if j == 8:
                    act_transposes(1)
                    pe.wait_ge(xg_in, k * 16 + 32)
                    xg_transposes()
            pe.wait_ge(xgT_ready, k * 2 + 4)

    ctx.close()
    return nc


_INS = ['x', 'mem', 't5_table', 'lb_logits', 'norm_mix', 'w_in', 'b_gates', 'hg_norm_gain', 'swa_sinks', 'w_branch_a',
        'w_branch_b', 'w_mix_out', 'norm_xa', 'xa_w_q', 'xa_w_k', 'xa_w_v', 'xa_w_o', 'norm_ffn', 'w_router',
        'b_router', 'w_gate_up', 'b_gate_up', 'w_down', 'b_down', 'norm_final']


def kernel(**inputs):
    import numpy as _np
    import concourse.bacc as _bacc
    from concourse import mybir as _mybir
    from concourse.bass_utils import run_bass_kernel_spmd as _run

    nc = _bacc.Bacc("TRN2", target_bir_lowering=False, num_devices=1)
    arrays, args = {}, []
    for name in _INS:
        a = _np.ascontiguousarray(inputs[name])
        arrays[f"in_{name}_dram"] = a
        args.append(nc.dram_tensor(f"in_{name}_dram", a.shape, _mybir.dt.from_np(a.dtype), kind="ExternalInput").ap())
    out = nc.dram_tensor("out_0_dram", (1, T, D), F32, kind="ExternalOutput").ap()
    build(nc, *args, out)
    r = _run(nc, [arrays], core_ids=[0])
    return r.results[0]["out_0_dram"]
```
